# Optimizing a Trainium2 kernel written in Bass

```python
import math
import jax, jax.numpy as jnp
from jax import lax
import numpy as np

D_MODEL = 2048
BATCH = 1
SEQ = 256
DEPTH = 2

CHUNK = 64
Q_BLOCK = 128

A_HEADS = 16
A_KV_HEADS = 2
A_HEAD_DIM = 64
A_WINDOW = 128
A_WIN_CHUNKS = A_WINDOW // CHUNK

B_HEADS = 8
B_NOPE = 128
B_ROPE = 64
B_V = 128
B_Q_RANK = 512
B_KV_RANK = 256
ROPE_THETA = 10000.0

C_HEADS = 16
C_HEAD_DIM = 128

D_FF = -(-8 * D_MODEL // (3 * 256)) * 256

ALPHA = (2 * DEPTH) ** 0.25
BETA = (8 * DEPTH) ** -0.25
LN_EPS = 1e-5
RMS_EPS = 1e-6

N_EVEN = (DEPTH + 1) // 2
N_ODD = DEPTH // 2

A_Q = A_HEADS * A_HEAD_DIM
A_KV = A_KV_HEADS * A_HEAD_DIM
EVEN_SPLITS = [A_Q, A_Q + A_KV, A_Q + 2 * A_KV, A_Q + 2 * A_KV + B_Q_RANK,
               A_Q + 2 * A_KV + B_Q_RANK + B_KV_RANK]
EVEN_IN = A_Q + 2 * A_KV + B_Q_RANK + B_KV_RANK + B_ROPE
EVEN_MIX = A_Q + B_HEADS * B_V
C_HD = C_HEADS * C_HEAD_DIM
ODD_IN = 3 * C_HD + C_HEADS
ODD_MIX = C_HD

kernel_name = "hybrid_swa_mla_fox_deepnorm_trunk"

F32 = jnp.float32

def layer_norm(x, g, b):
    xf = x.astype(F32)
    mu = jnp.mean(xf, axis=-1, keepdims=True)
    var = jnp.mean(jnp.square(xf - mu), axis=-1, keepdims=True)
    y = (xf - mu) * lax.rsqrt(var + LN_EPS) * g.astype(F32) + b.astype(F32)
    return y.astype(x.dtype)

def rms_norm(x, g):
    xf = x.astype(F32)
    y = xf * lax.rsqrt(jnp.mean(jnp.square(xf), axis=-1, keepdims=True) + RMS_EPS) * g.astype(F32)
    return y.astype(x.dtype)

def alibi_slopes(n_heads):
    return jnp.exp2(-8.0 * (jnp.arange(n_heads, dtype=F32) + 1.0) / n_heads)

def rope_tables(seq, dtype):
    inv_freq = ROPE_THETA ** (-jnp.arange(0, B_ROPE, 2, dtype=F32) / B_ROPE)
    ang = jnp.arange(seq, dtype=F32)[:, None] * inv_freq[None, :]
    return jnp.cos(ang).astype(dtype), jnp.sin(ang).astype(dtype)

def apply_rope(x, cos, sin):
    x1, x2 = jnp.split(x, 2, axis=-1)
    return jnp.concatenate([x1 * cos - x2 * sin, x2 * cos + x1 * sin], axis=-1)

def sliding_sink_attention(q, k, v, sinks):
    B, S = q.shape[0], q.shape[1]
    nC = S // CHUNK
    G = A_HEADS // A_KV_HEADS
    W = A_WIN_CHUNKS
    qc = q.reshape(B, nC, CHUNK, A_KV_HEADS, G, A_HEAD_DIM)
    kc = k.reshape(B, nC, CHUNK, A_KV_HEADS, A_HEAD_DIM)
    vc = v.reshape(B, nC, CHUNK, A_KV_HEADS, A_HEAD_DIM)

    def band(t):
        pad = jnp.pad(t, ((0, 0), (W - 1, 0), (0, 0), (0, 0), (0, 0)))
        return jnp.concatenate([pad[:, j:j + nC] for j in range(W)], axis=2)

    kb, vb = band(kc), band(vc)
    s = jnp.einsum('bcqhgd,bckhd->bchgqk', qc, kb, preferred_element_type=F32) * (A_HEAD_DIM ** -0.5)
    qi = jnp.arange(CHUNK)
    ki = jnp.arange(W * CHUNK)
    dist = jnp.abs((W - 1) * CHUNK + qi[:, None] - ki[None, :]).astype(F32)
    alibi = -alibi_slopes(A_HEADS).reshape(A_KV_HEADS, G, 1, 1) * dist
    valid = (jnp.arange(nC)[:, None] * CHUNK + ki[None, :]) >= (W - 1) * CHUNK
    s = jnp.where(valid[None, :, None, None, None, :], s + alibi, -jnp.inf)
    sink = jnp.broadcast_to(sinks.astype(F32).reshape(1, 1, A_KV_HEADS, G, 1, 1), s.shape[:-1] + (1,))
    p = jax.nn.softmax(jnp.concatenate([s, sink], axis=-1), axis=-1)[..., :-1].astype(v.dtype)
    o = jnp.einsum('bchgqk,bckhd->bcqhgd', p, vb)
    return o.reshape(B, S, A_Q)

def to_blocks(t):
    B, S = t.shape[0], t.shape[1]
    return jnp.moveaxis(t.reshape((B, S // Q_BLOCK, Q_BLOCK) + t.shape[2:]), 1, 0)

def from_blocks(t):
    t = jnp.moveaxis(t, 0, 1)
    return t.reshape((t.shape[0], t.shape[1] * t.shape[2]) + t.shape[3:])

def mla_attention(q_nope, q_rope, k_nope, k_rope, v):
    B, S = q_nope.shape[0], q_nope.shape[1]
    scale = (B_NOPE + B_ROPE) ** -0.5
    k_chunk = jnp.arange(S) // CHUNK

    def block(args):
        qn, qr, i = args
        s = (jnp.einsum('bqhd,bkhd->bhqk', qn, k_nope, preferred_element_type=F32)
             + jnp.einsum('bqhd,bkd->bhqk', qr, k_rope, preferred_element_type=F32)) * scale
        q_chunk = (i * Q_BLOCK + jnp.arange(Q_BLOCK)) // CHUNK
        s = jnp.where(k_chunk[None, :] <= q_chunk[:, None], s, -jnp.inf)
        p = jax.nn.softmax(s, axis=-1).astype(v.dtype)
        return jnp.einsum('bhqk,bkhd->bqhd', p, v)

    out = lax.map(block, (to_blocks(q_nope), to_blocks(q_rope), jnp.arange(S // Q_BLOCK)))
    return from_blocks(out).reshape(B, S, B_HEADS * B_V)

def forgetting_attention(q, k, v, log_f):
    B, S = q.shape[0], q.shape[1]
    scale = C_HEAD_DIM ** -0.5
    cum = lax.cumsum(log_f, axis=1)
    cum_k = jnp.transpose(cum, (0, 2, 1))
    k_pos = jnp.arange(S)

    def block(args):
        qb, cq, i = args
        s = jnp.einsum('bqhd,bkhd->bhqk', qb, k, preferred_element_type=F32) * scale
        s = s + (jnp.transpose(cq, (0, 2, 1))[..., None] - cum_k[:, :, None, :])
        t = i * Q_BLOCK + jnp.arange(Q_BLOCK)
        s = jnp.where(k_pos[None, :] <= t[:, None], s, -jnp.inf)
        p = jax.nn.softmax(s, axis=-1).astype(v.dtype)
        return jnp.einsum('bhqk,bkhd->bqhd', p, v)

    out = lax.map(block, (to_blocks(q), to_blocks(cum), jnp.arange(S // Q_BLOCK)))
    return from_blocks(out).reshape(B, S, C_HD)

def even_mixer(x, w_in, sinks, q_norm, w_uq, kv_norm, w_ukv, w_out, cos, sin):
    B, S, _ = x.shape
    h = x @ w_in
    q_a, k_a, v_a, c_q, c_kv, k_r = jnp.split(h, EVEN_SPLITS, axis=-1)
    o_a = sliding_sink_attention(q_a.reshape(B, S, A_HEADS, A_HEAD_DIM),
                                 k_a.reshape(B, S, A_KV_HEADS, A_HEAD_DIM),
                                 v_a.reshape(B, S, A_KV_HEADS, A_HEAD_DIM), sinks)
    q = (rms_norm(c_q, q_norm) @ w_uq).reshape(B, S, B_HEADS, B_NOPE + B_ROPE)
    q_nope, q_rope = q[..., :B_NOPE], apply_rope(q[..., B_NOPE:], cos[None, :, None, :], sin[None, :, None, :])
    kv = (rms_norm(c_kv, kv_norm) @ w_ukv).reshape(B, S, B_HEADS, B_NOPE + B_V)
    k_nope, v_b = kv[..., :B_NOPE], kv[..., B_NOPE:]
    k_rope = apply_rope(k_r, cos[None], sin[None])
    o_b = mla_attention(q_nope, q_rope, k_nope, k_rope, v_b)
    return jnp.concatenate([o_a, o_b], axis=-1) @ w_out

def odd_mixer(x, w_in, forget_bias, w_out):
    B, S, _ = x.shape
    h = x @ w_in
    q = h[..., :C_HD].reshape(B, S, C_HEADS, C_HEAD_DIM)
    k = h[..., C_HD:2 * C_HD].reshape(B, S, C_HEADS, C_HEAD_DIM)
    v = h[..., 2 * C_HD:3 * C_HD].reshape(B, S, C_HEADS, C_HEAD_DIM)
    log_f = jax.nn.log_sigmoid((h[..., 3 * C_HD:] + forget_bias).astype(F32))
    return forgetting_attention(q, k, v, log_f) @ w_out

def swiglu(x, w_gate, w_up, w_down):
    return (jax.nn.silu(x @ w_gate) * (x @ w_up)) @ w_down

def setup_inputs(seed: int = 0) -> dict:
    key = jax.random.key(seed)
    ks = jax.random.split(key, 20)
    nrm = lambda k, shape, s: jax.random.normal(k, shape, F32) * s
    return {
        "x": nrm(ks[0], (BATCH, SEQ, D_MODEL), 1.0),
        "even_w_in": nrm(ks[1], (N_EVEN, D_MODEL, EVEN_IN), D_MODEL ** -0.5),
        "even_sinks": nrm(ks[2], (N_EVEN, A_HEADS), 1.0),
        "even_q_norm": 1.0 + nrm(ks[3], (N_EVEN, B_Q_RANK), 0.02),
        "even_w_uq": nrm(ks[4], (N_EVEN, B_Q_RANK, B_HEADS * (B_NOPE + B_ROPE)), B_Q_RANK ** -0.5),
        "even_kv_norm": 1.0 + nrm(ks[5], (N_EVEN, B_KV_RANK), 0.02),
        "even_w_ukv": nrm(ks[6], (N_EVEN, B_KV_RANK, B_HEADS * (B_NOPE + B_V)), B_KV_RANK ** -0.5),
        "even_w_out": nrm(ks[7], (N_EVEN, EVEN_MIX, D_MODEL), BETA * EVEN_MIX ** -0.5),
        "odd_w_in": nrm(ks[8], (N_ODD, D_MODEL, ODD_IN), D_MODEL ** -0.5),
        "odd_forget_bias": jnp.linspace(1.0, 5.0, C_HEADS, dtype=F32)[None, :] + nrm(ks[9], (N_ODD, C_HEADS), 0.1),
        "odd_w_out": nrm(ks[10], (N_ODD, ODD_MIX, D_MODEL), BETA * ODD_MIX ** -0.5),
        "ffn_w_gate": nrm(ks[11], (DEPTH, D_MODEL, D_FF), D_MODEL ** -0.5),
        "ffn_w_up": nrm(ks[12], (DEPTH, D_MODEL, D_FF), D_MODEL ** -0.5),
        "ffn_w_down": nrm(ks[13], (DEPTH, D_FF, D_MODEL), BETA * D_FF ** -0.5),
        "ln_gain": 1.0 + nrm(ks[14], (DEPTH, 2, D_MODEL), 0.02),
        "ln_bias": nrm(ks[15], (DEPTH, 2, D_MODEL), 0.02),
    }

def reference(x, even_w_in, even_sinks, even_q_norm, even_w_uq, even_kv_norm, even_w_ukv, even_w_out,
              odd_w_in, odd_forget_bias, odd_w_out, ffn_w_gate, ffn_w_up, ffn_w_down, ln_gain, ln_bias):
    cos, sin = rope_tables(x.shape[1], x.dtype)
    for layer in range(DEPTH):
        i = layer // 2
        if layer % 2 == 0:
            y = even_mixer(x, even_w_in[i], even_sinks[i], even_q_norm[i], even_w_uq[i],
                           even_kv_norm[i], even_w_ukv[i], even_w_out[i], cos, sin)
        else:
            y = odd_mixer(x, odd_w_in[i], odd_forget_bias[i], odd_w_out[i])
        x = layer_norm(ALPHA * x + y, ln_gain[layer, 0], ln_bias[layer, 0])
        x = layer_norm(ALPHA * x + swiglu(x, ffn_w_gate[layer], ffn_w_up[layer], ffn_w_down[layer]),
                       ln_gain[layer, 1], ln_bias[layer, 1])
    return x


_drawn_inputs = setup_inputs


def setup_inputs(seed=0):
    import zlib

    import numpy as np

    out = dict(_drawn_inputs(seed))
    spreads = {}
    factors = {'even_sinks': 6.2, 'even_q_norm': 8.0, 'even_kv_norm': 8.0}
    for name, (base, spread) in spreads.items():
        noise = np.random.default_rng([zlib.crc32(name.encode()), seed]).standard_normal(out[name].shape)
        drawn = base * np.exp(spread * noise) if base else spread * noise
        out[name] = __import__('jax').numpy.asarray(drawn.astype(out[name].dtype))
    for name, factor in factors.items():
        out[name] = (out[name] * factor).astype(out[name].dtype)
    return out
```

```python
from contextlib import ExitStack, contextmanager

import numpy as np

import concourse.bass as bass
from concourse import mybir

F32 = mybir.dt.float32
F32R = mybir.dt.float32r
ALU = mybir.AluOpType
ACT = mybir.ActivationFunctionType
AX_X = mybir.AxisListType.X

P = 128
D = 2048
KT = D // P
S = 256
TT = S // P
N = 512
DEPTH = 2
D_FF = 5632
FT = D_FF // P
FSTRIPS = D_FF // N
ALPHA = (2 * DEPTH) ** 0.25
LN_EPS = 1e-5
RMS_EPS = 1e-6

A_HEADS, A_KV, A_DIM = 16, 2, 64
B_HEADS, B_NOPE, B_ROPE, B_V = 8, 128, 64, 128
B_QR, B_KVR = 512, 256
C_HEADS, C_DIM = 16, 128
CHUNK = 64
A_Q = A_HEADS * A_DIM
KA0 = A_Q
VA0 = KA0 + A_KV * A_DIM
CQ0 = VA0 + A_KV * A_DIM
CKV0 = CQ0 + B_QR
KR0 = CKV0 + B_KVR
EVEN_IN = KR0 + B_ROPE
C_HD = C_HEADS * C_DIM
ODD_IN = 3 * C_HD + C_HEADS
GROUPS = C_HD // N
GH = N // C_DIM
HEADS_EVEN = A_HEADS + B_HEADS
MIX_A = A_HEADS // 2
PAIRS = B_HEADS // 2
BIG = 1e30

SLOTS = 4
AHEAD = 3
LAG = 3
UQW = 2 * (B_NOPE + B_ROPE)

C_ID, C_U, C_ONE, C_G, C_MC, C_DA, C_MB, C_COS, C_SIN, C_SL = np.cumsum([0, P, P, P, P, 3 * P, 3 * P, 3 * P, P, P]).tolist()
C_END = C_SL + A_HEADS


def constants():
    c = np.zeros((P, C_END), np.float32)
    r = np.arange(P)
    c[:, C_ID:C_ID + P] = np.eye(P)
    c[:, C_U:C_U + P] = r[:, None] <= r[None, :]
    c[:, C_ONE:C_ONE + P] = 1
    c[:, C_G:C_G + P] = r[:, None] > r[None, :]
    pairs = [(0, 0), (1, 0), (1, 1)]
    for n, (tq, tk) in enumerate(pairs):
        q, k = tq * P + r[:, None], tk * P + r[None, :]
        cq, ck = q // CHUNK, k // CHUNK
        at = slice(n * P, (n + 1) * P)
        c[:, C_MC:C_DA][:, at] = np.where(k <= q, 0, -BIG)
        c[:, C_DA:C_MB][:, at] = np.where((ck <= cq) & (ck >= cq - 1), np.abs(q - k), BIG)
        c[:, C_MB:C_COS][:, at] = np.where(ck <= cq, 0, -BIG)
    inv = (10000.0 ** (-np.arange(0, B_ROPE, 2, dtype=np.float32) / np.float32(B_ROPE))).astype(np.float32)
    ang = np.arange(S, dtype=np.float32)[:, None] * inv[None, :]
    for at, f in ((C_COS, np.cos), (C_SIN, np.sin)):
        t = f(ang).astype(np.float32).reshape(TT, P, 1, B_ROPE // 2).transpose(1, 0, 2, 3)
        c[:, at:at + P] = np.broadcast_to(t, (P, TT, 2, B_ROPE // 2)).reshape(P, P)
    c[:, C_SL:C_END] = -np.exp2(-8.0 * (np.arange(A_HEADS, dtype=np.float32) + 1) / A_HEADS)
    return c


class Tally:

    def __init__(self):
        self.value, self.i, self.times = 0, None, 1

    def enter(self, i, first, times, per):
        self.i, self.first, self.times, self.per, self.start = i, first, times, per, self.value

    def leave(self):
        assert self.value == self.start + self.per, (self.value, self.start, self.per)
        self.value = self.start + self.per * self.times
        self.i, self.times, self.per = None, 1, 0

    def now(self, more=0):
        if self.i is None or not self.per:
            return self.value + more
        return self.i * self.per + (self.value - self.first * self.per + more)

    def rounds(self):
        return [self.value + m * self.per for m in range(self.times)] if self.i is not None else [self.value]

    def tick(self, n=1):
        self.value += n


@contextmanager
def repeated(engine, tallies, first, end, **per):
    with engine.Fori(first, end) as i:
        for name, t in tallies.items():
            t.enter(i, first, end - first, per.get(name, 0))
        yield i
    for t in tallies.values():
        t.leave()


class Plan:

    def __init__(self):
        self.units = []
        strips = [(KT, CQ0 - KA0, 1), (KT, N, 1), (KT, N, 1), (KT, EVEN_IN - CKV0, 1), (KT, N, 1)]
        strips += [(B_KVR // P, N, 0)] * PAIRS + [(B_QR // P, UQW, 0)] * PAIRS
        ffn = [(KT, N, 1)] * (2 * FSTRIPS) + [(FT, N, 1)] * (D // N)
        strips += [(KT, N, 1)] * (D // N) + ffn + [(KT, N, 1)] * (3 * GROUPS + D // N) + ffn
        slot = load = 0
        last_in_slot, last_in_load, uses = {}, {}, [0] * SLOTS
        for kts, width, fresh in strips:
            if fresh:
                slot = load = 0
            for k in range(0, kts, 2):
                u = len(self.units)
                x = dict(slot=slot, back=u - last_in_slot[slot] if slot in last_in_slot else None,
                         width=width, half=k // 2 % 2, load=load)
                if k % 4 == 0:
                    x["load_back"] = u - last_in_load[load] if load in last_in_load else None
                    uses[load] += 1
                    x["uses"] = uses[load]
                self.units.append(x)
                last_in_slot[slot] = u
                last_in_load[load] = u
                slot = (slot + 1) % SLOTS
                if k % 4 == 2 or k + 2 >= kts:
                    load = (load + 1) % SLOTS

    def get(self, tally, key, more=0):
        found = [self.units[u + more][key] for u in tally.rounds()]
        assert len(set(found)) == 1, (key, found)
        return found[0]

    def nearest(self, tally, key, more=0):
        found = [self.units[u + more][key] for u in tally.rounds()]
        return min(x for x in found if x is not None) if any(x is not None for x in found) else None


PLAN = Plan()
UNITS = len(PLAN.units)


def trunk(nc, x_in, even_w_in, even_sinks, even_q_norm, even_w_uq, even_kv_norm, even_w_ukv, even_w_out,
          odd_w_in, odd_forget_bias, odd_w_out, ffn_w_gate, ffn_w_up, ffn_w_down, ln_gain, ln_bias, consts, out):
    ctx = ExitStack()
    with ctx:
        def sb(name, shape, dt=F32):
            return ctx.enter_context(nc.sbuf_tensor(name, shape, dt))

        def overlaid(*tensors):
            with ExitStack() as room:
                return [room.enter_context(nc.sbuf_tensor(*t)) for t in tensors]

        def sem(name):
            return ctx.enter_context(nc.semaphore(name))

        raw = sb("raw", [P, SLOTS, 4, N])
        w_high = sb("w_high", [P, SLOTS, 2, N], F32R)
        w_low = sb("w_low", [P, SLOTS, 2, N], F32R)
        x = sb("x", [P, TT, D])
        work = sb("work", [P, 2, N])
        ident = sb("ident", [P, P])
        ln_cols = sb("ln_cols", [P, 2 * DEPTH * 2 * KT])
        rms_cols = sb("rms_cols", [P, (B_QR + B_KVR) // P])
        stats = sb("stats", [P, TT, D // N, 6])
        moments = sb("moments", [P, TT, 2])
        var_eps = sb("var_eps", [P, TT])
        rstd = sb("rstd", [P, TT])
        minus_mean = sb("minus_mean", [P, 1])
        rms_sum = sb("rms_sum", [P, TT])
        minus_half = sb("minus_half", [P, TT])
        row_max = sb("row_max", [P, 2, TT])
        row_sum = sb("row_sum", [P, 2, TT])
        row_inv = sb("row_inv", [P, 2, TT])
        (ln_rows_end,) = overlaid(("ln_rows_end", [P, 2, D], F32))
        vb, qTn, kTn, qTr = overlaid(
            ("vb", [P, TT, B_HEADS, B_V], F32), ("qTn", [P, B_HEADS, S], F32), ("kTn", [P, B_HEADS, S], F32),
            ("qTr", [P, PAIRS, S], F32))
        xT_high = sb("xT_high", [P, KT, S], F32R)
        xT_low = sb("xT_low", [P, KT, S], F32R)
        hid_high, hid_low = overlaid(("hid_high", [P, FT, S], F32R), ("hid_low", [P, FT, S], F32R))
        room_h = 2 * FT * S
        _, ln_rows = overlaid(("ln_rows_before", [P, room_h - 2 * D], F32), ("ln_rows", [P, 2, D], F32))
        both = [("probs", [P, 2, 3 * P + 2], F32), ("probsT", [P, 2, 3 * P], F32), ("nat", [P, TT, N], F32),
                ("mixT_high", [P, KT, S], F32R), ("mixT_low", [P, KT, S], F32R)]
        with ExitStack() as shared:
            probs, probsT, nat, mixT_high, mixT_low = [shared.enter_context(nc.sbuf_tensor(*t)) for t in both]
            (cqT_high, cqT_low, ckvT_high, ckvT_low, qTa, kTa, va, kan, qn, roped, krn, kbn, kTr, dist_a, mask_b,
             cos_t, sin_t, slopes, sinks, rope_tmp, vec_rows, rms_rows) = overlaid(
                ("cqT_high", [P, B_QR // P, S], F32R), ("cqT_low", [P, B_QR // P, S], F32R),
                ("ckvT_high", [P, B_KVR // P, S], F32R), ("ckvT_low", [P, B_KVR // P, S], F32R),
                ("qTa", [P, MIX_A, S], F32), ("kTa", [P, A_KV, S], F32), ("va", [P, TT, P], F32),
                ("kan", [P, TT, A_KV, 2, A_DIM], F32), ("qn", [P, TT, 2, B_NOPE + B_ROPE], F32),
                ("roped", [P, TT, 2, B_ROPE], F32), ("krn", [P, TT, 2, B_ROPE], F32),
                ("kbn", [P, TT, 2, B_NOPE], F32), ("kTr", [P, S], F32),
                ("dist_a", [P, 3 * P], F32), ("mask_b", [P, 3 * P], F32), ("cos_t", [P, P], F32),
                ("sin_t", [P, P], F32), ("slopes", [P, A_HEADS], F32), ("sinks", [P, A_HEADS], F32),
                ("rope_tmp", [P, 4, TT, 2, B_ROPE // 2], F32), ("vec_rows", [P, P], F32),
                ("rms_rows", [(B_QR + B_KVR) // P, P], F32))
            (qTc, kTc, vc, tri, ones_late, mask_c, decay, gate_raw, gate_high, gate_low, log_f, log_f_high,
             log_f_low, gate_tmp, group_f, f_bias) = overlaid(
                ("qTc", [P, GH, S], F32), ("kTc", [P, GH, S], F32), ("vc", [P, TT, N], F32),
                ("tri", [P, 4 * P], F32), ("ones_late", [P, 2 * P], F32R), ("mask_c", [P, 3 * P], F32),
                ("decay", [P, 2, 2, 3, P], F32R),
                ("gate_raw", [P, KT, C_HEADS], F32), ("gate_high", [P, KT, C_HEADS], F32R),
                ("gate_low", [P, KT, C_HEADS], F32R),
                ("log_f", [P, TT, C_HEADS], F32), ("log_f_high", [P, TT, C_HEADS], F32R),
                ("log_f_low", [P, TT, C_HEADS], F32), ("gate_tmp", [P, 4, TT, C_HEADS], F32),
                ("group_f", [P, 2, TT, GH], F32), ("f_bias", [P, C_HEADS], F32))

        acc = [[ctx.enter_context(nc.psum_tensor(f"acc{s}{t}", [P, N], F32)) for t in range(TT)] for s in range(2)]
        aux = [ctx.enter_context(nc.psum_tensor(f"aux{b}", [P, N], F32)) for b in range(4)]
        SCORES, PROBS, MIX, TURN = aux

        landed = [sem(f"landed{s}") for s in range(SLOTS)]
        rounded = sem("rounded")
        cut = sem("cut")
        multiplied = sem("multiplied")
        acc_read = [sem(f"acc_read{s}") for s in range(2)]
        turned = sem("turned")
        turn_read = sem("turn_read")
        work_cut = sem("work_cut")
        work_high = sem("work_high")
        half_multiplied = sem("half_multiplied")
        end_shift = sem("end_shift")
        end_scaled = sem("end_scaled")
        end_second = sem("end_second")
        first_in = sem("first_in")
        x_landed = [sem(f"x_landed{c}") for c in range(D // N)]
        even_in = sem("even_in")
        odd_in = sem("odd_in")
        cols_made = sem("cols_made")
        half_set = sem("half_set")
        vector_self = sem("vector_self")
        var_ready = sem("var_ready")
        rstd_ready = sem("rstd_ready")
        squares = sem("squares")
        normed = sem("normed")
        rows_in = sem("rows_in")
        affine = sem("affine")
        pool_self = sem("pool_self")
        keys_dup = sem("keys_dup")
        rope_done = sem("rope_done")
        scores_made = sem("scores_made")
        scores_read = sem("scores_read")
        maxed = sem("maxed")
        exped = sem("exped")
        summed = sem("summed")
        probs_made = sem("probs_made")
        sink_set = sem("sink_set")
        probs_turned = sem("probs_turned")
        probsT_made = sem("probsT_made")
        mixed = sem("mixed")
        mix_rounded = sem("mix_rounded")
        mix_read = sem("mix_read")
        gate_rounded = sem("gate_rounded")
        gate_cut = sem("gate_cut")
        gates_made = sem("gates_made")
        gate_bias = sem("gate_bias")
        gate_abs = sem("gate_abs")
        gate_ln = sem("gate_ln")
        forget_ready = sem("forget_ready")
        ones_ready = sem("ones_ready")
        decay_ready = sem("decay_ready")
        hid_rounded = sem("hid_rounded")
        stored = sem("stored")

        w_in_v = even_w_in[0].rearrange("(k p) n -> p k n", p=P)
        w_uq_v = even_w_uq[0].rearrange("(k p) n -> p k n", p=P)
        w_ukv_v = even_w_ukv[0].rearrange("(k p) n -> p k n", p=P)
        w_eo_v = even_w_out[0].rearrange("(k p) n -> p k n", p=P)
        w_oin_v = odd_w_in[0].rearrange("(k p) n -> p k n", p=P)
        w_oo_v = odd_w_out[0].rearrange("(k p) n -> p k n", p=P)
        w_gate_v = [ffn_w_gate[i].rearrange("(k p) n -> p k n", p=P) for i in range(DEPTH)]
        w_up_v = [ffn_w_up[i].rearrange("(k p) n -> p k n", p=P) for i in range(DEPTH)]
        w_down_v = [ffn_w_down[i].rearrange("(k p) n -> p k n", p=P) for i in range(DEPTH)]
        x_v = x_in[0].rearrange("(t p) d -> p t d", p=P)
        out_v = out[0].rearrange("(t p) d -> p t d", p=P)

        MIX_EVEN = MIX_A + B_HEADS
        HALF_UNITS = KT // 2
        DOWN_UNITS = FT // 2
        UQ_AT = PAIRS
        OUT_AT = 3 * PAIRS
        HEADS_AT = UQ_AT + 5

        block = ctx.enter_context(nc.Block())

        @block.sync
        def _(sp):
            units = Tally()
            tallies = {"units": units}

            def fetch(src, k0, k1, cols, width):
                back = PLAN.nearest(units, "load_back")
                if back is not None:
                    sp.wait_ge(cut, units.now(1 - back))
                slot = PLAN.get(units, "load")
                sp.dma_start(raw[:, slot, 0:k1 - k0, 0:width], src[:, k0:k1, cols]).then_inc(landed[slot], 16)
                units.tick((k1 - k0) // 2)

            def strip(src, kts, cols, width=N):
                for k0 in range(0, kts, 4):
                    fetch(src, k0, min(k0 + 4, kts), cols, width)

            def ln_vectors(k, rows, to):
                sp.dma_start(to[:, 0, :], ln_gain[k // 2, k % 2:k % 2 + 1, :].to_broadcast([P, D])).then_inc(rows, 16)
                sp.dma_start(to[:, 1, :], ln_bias[k // 2, k % 2:k % 2 + 1, :].to_broadcast([P, D])).then_inc(rows, 16)

            def projection(src):
                for s in range(D // N):
                    strip(src, KT, slice(s * N, (s + 1) * N))

            def swiglu(layer):
                strip(w_gate_v[layer], KT, slice(0, N))
                sp.wait_ge(multiplied, units.now(-HALF_UNITS))
                ln_vectors(2 * layer, rows_in, ln_rows)
                strip(w_up_v[layer], KT, slice(0, N))
                with repeated(sp, tallies, 1, FSTRIPS, units=2 * HALF_UNITS) as i:
                    strip(w_gate_v[layer], KT, bass.ds(i * N, N))
                    strip(w_up_v[layer], KT, bass.ds(i * N, N))
                if layer == DEPTH - 1:
                    strip(w_down_v[layer], FT, slice(0, N))
                    sp.wait_ge(multiplied, units.now(-DOWN_UNITS))
                    ln_vectors(2 * layer + 1, rows_in, ln_rows_end)
                    for s in range(1, D // N):
                        strip(w_down_v[layer], FT, slice(s * N, (s + 1) * N))
                else:
                    with repeated(sp, tallies, 0, D // N // 2, units=2 * DOWN_UNITS) as i:
                        for s in range(2):
                            strip(w_down_v[layer], FT, bass.ds(i * (2 * N) + s * N, N))

            sp.dma_start(ident[:, :], consts[:, C_ID:C_ID + P]).then_inc(first_in, 16)
            for c in range(D // N):
                sp.dma_start(x[:, :, c * N:(c + 1) * N], x_v[:, :, c * N:(c + 1) * N]).then_inc(x_landed[c], 16)
                fetch(w_in_v, 4 * c, 4 * c + 4, slice(KA0, CQ0), CQ0 - KA0)
            n_vec = DEPTH * 2 * KT
            sp.dma_start(vec_rows[0:n_vec, :], ln_gain.rearrange("l s (k p) -> (l s k) p", p=P)).then_inc(first_in, 16)
            sp.dma_start(vec_rows[n_vec:2 * n_vec, :], ln_bias.rearrange("l s (k p) -> (l s k) p", p=P)).then_inc(first_in, 16)
            sp.dma_start(rms_rows[0:B_QR // P, :], even_q_norm.rearrange("a (k p) -> (a k) p", p=P)).then_inc(first_in, 16)
            sp.dma_start(rms_rows[B_QR // P:, :], even_kv_norm.rearrange("a (k p) -> (a k) p", p=P)).then_inc(first_in, 16)
            for to, at in ((dist_a, C_DA), (mask_b, C_MB), (cos_t, C_COS), (sin_t, C_SIN), (slopes, C_SL)):
                sp.dma_start(to[:, :], consts[:, at:at + to.shape[1]]).then_inc(even_in, 16)
            sp.dma_start(sinks[:, :], even_sinks[0:1, :].to_broadcast([P, A_HEADS])).then_inc(even_in, 16)
            strip(w_in_v, KT, slice(0, N))
            strip(w_in_v, KT, slice(N, 2 * N))
            strip(w_in_v, KT, slice(CKV0, EVEN_IN), EVEN_IN - CKV0)
            strip(w_in_v, KT, slice(CQ0, CKV0))
            for p in range(PAIRS):
                strip(w_ukv_v, B_KVR // P, slice(p * N, (p + 1) * N))
            for p in range(PAIRS):
                strip(w_uq_v, B_QR // P, slice(p * UQW, (p + 1) * UQW), UQW)
            projection(w_eo_v)
            swiglu(0)
            strip(w_oin_v, KT, slice(0, N))
            sp.wait_ge(multiplied, units.now(-HALF_UNITS))
            ln_vectors(1, rows_in, ln_rows)
            sp.dma_start(gate_raw[:, :, :], w_oin_v[:, :, 3 * C_HD:ODD_IN]).then_inc(odd_in, 16)
            sp.dma_start(tri[:, :], consts[:, C_U:C_U + 4 * P]).then_inc(odd_in, 16)
            sp.dma_start(mask_c[:, :], consts[:, C_MC:C_MC + 3 * P]).then_inc(odd_in, 16)
            sp.dma_start(f_bias[:, :], odd_forget_bias[0:1, :].to_broadcast([P, C_HEADS])).then_inc(odd_in, 16)
            strip(w_oin_v, KT, slice(C_HD, C_HD + N))
            strip(w_oin_v, KT, slice(2 * C_HD, 2 * C_HD + N))
            with repeated(sp, tallies, 1, GROUPS, units=3 * HALF_UNITS) as i:
                for part in range(3):
                    strip(w_oin_v, KT, bass.ds(i * N + part * C_HD, N))
            projection(w_oo_v)
            swiglu(1)
            assert units.value == UNITS
            for c in range(D // N):
                cols = slice(c * N, (c + 1) * N)
                sp.wait_ge(affine, 3 + c + 1)
                sp.dma_start(out_v[:, 0, cols], x[:, 0, cols]).then_inc(stored, 16)
                sp.wait_ge(end_second, c + 1)
                sp.dma_start(out_v[:, 1, cols], x[:, 1, cols]).then_inc(stored, 16)
            sp.wait_ge(stored, 16 * TT * (D // N))

        @block.tensor
        def _(pe):
            units, turns, sets = Tally(), Tally(), [Tally(), Tally()]
            tallies = {"units": units, "turns": turns, "set0": sets[0], "set1": sets[1]}

            def products(high, low, kts, s, width=N, gap=None, halves=False):
                for k in range(0, kts, 2):
                    if gap:
                        gap(k // 2)
                    if k == 0 and sets[s].value:
                        pe.wait_ge(acc_read[s], sets[s].now() * TT)
                    pe.wait_ge(cut, units.now(1))
                    slot = PLAN.get(units, "slot")
                    for t in range(TT):
                        rows = slice(t * P, (t + 1) * P)
                        for r in range(2):
                            for n, (a, b) in enumerate(((high, w_high), (high, w_low), (low, w_high))):
                                mm = pe.matmul(acc[s][t][:, 0:width], a[:, k + r, rows], b[:, slot, r, 0:width],
                                               start=(k + r == 0 and n == 0), stop=(k + r == kts - 1 and n == 2))
                        if halves and t == 0 and k + 2 == kts:
                            mm.then_inc(half_multiplied, 1)
                    mm.then_inc(multiplied, 1)
                    units.tick()
                sets[s].tick()

            def turn(pieces, bank=TURN, banks=1):
                if turns.value >= banks:
                    pe.wait_ge(turn_read, turns.now(1 - banks))
                for src, at in pieces:
                    tr = pe.transpose(bank[:, at:at + P], src, ident[:, :])
                tr.then_inc(turned, 1)
                turns.tick()

            def turn_rows(src, k0, count, **bank):
                turn([(src[:, t, (k0 + r) * P:(k0 + r + 1) * P], r * S + t * P) for r in range(count) for t in range(TT)],
                     **bank)

            def turning(chunks, cut_before, lead=3):
                def batch(b):
                    if chunks is None:
                        pe.wait_ge(x_landed[b // 2], 16)
                    else:
                        pe.wait_ge(normed, chunks + b // 2 + 1)
                    turn_rows(x, 2 * b, 2, bank=aux[b % 4], banks=4)

                def gap(k):
                    for b in range(lead) if k == 0 else range(k + lead - 1, min(k + lead, KT // 2)):
                        batch(b)
                    pe.wait_ge(work_cut, cut_before + k + 1)
                return gap

            def scores(n, heads, first=False):
                if not first:
                    pe.wait_ge(scores_read, n)
                for t in range(TT):
                    at = slice(0, P) if t == 0 else slice(P, 3 * P)
                    for m, (q, k) in enumerate(heads):
                        mm = pe.matmul(SCORES[:, at], q[:, t * P:(t + 1) * P], k[:, 0:(t + 1) * P],
                                       start=(m == 0), stop=(m == len(heads) - 1))
                mm.then_inc(scores_made, 1)

            def turn_probs(n, parity, src, first=False):
                pe.wait_ge(probs_made, n + 1)
                if not first:
                    pe.wait_ge(probsT_made, n)
                for c in range(3):
                    tr = pe.transpose(PROBS[:, c * P:(c + 1) * P], src[:, parity, 1 + c * P:1 + (c + 1) * P], ident[:, :])
                tr.then_inc(probs_turned, 1)

            def mix(n, parity, src, values, m=None, rows=slice(0, P)):
                pe.wait_ge(probsT_made, n + 1)
                if m is not None:
                    pe.wait_ge(mix_read, m)
                pe.matmul(MIX[rows, 0:S], values[0], src[:, parity, 0:2 * P], start=True, stop=False)
                pe.matmul(MIX[rows, P:S], values[1], src[:, parity, 2 * P:3 * P], start=False, stop=True).then_inc(mixed, 1)

            def slot(s, first, count):
                h = first + s
                if s - 2 in range(count):
                    turn_probs(h - 2, h % 2, probs, first=(h == 2))
                if s < count:
                    if h < A_HEADS:
                        half = slice((h % 2) * A_DIM, (h % 2 + 1) * A_DIM)
                        heads = [(qTa[half, h // 2, :], kTa[half, h // (A_HEADS // A_KV), :])]
                    else:
                        b = h - A_HEADS
                        half = slice((b % 2) * B_ROPE, (b % 2 + 1) * B_ROPE)
                        heads = [(qTn[:, b, :], kTn[:, b, :]), (qTr[half, b // 2, :], kTr[half, :])]
                    if h % 4 == 0 or h >= A_HEADS:
                        pe.wait_ge(turn_read, turns.now())
                    scores(h, heads, first=(h == 0))
                h -= LAG
                if s - LAG in range(count):
                    if h < A_HEADS:
                        g = h // (A_HEADS // A_KV)
                        values = [va[:, t, g * A_DIM:(g + 1) * A_DIM] for t in range(TT)]
                        mix(h, h % 2, probsT, values, m=h // 2 if h % 2 == 0 and h else None,
                            rows=slice((h % 2) * A_DIM, (h % 2 + 1) * A_DIM))
                    else:
                        mix(h, h % 2, probsT, [vb[:, t, h - A_HEADS, :] for t in range(TT)], m=MIX_A + h - A_HEADS)

            pe.wait_ge(first_in, 16)
            products(xT_high, xT_low, KT, 0, CQ0 - KA0, turning(None, 0, 2))

            def gap(k):
                if k == 1:
                    pe.wait_ge(acc_read[0], sets[0].now() * TT)
                    turn([(kan[:, t, g, :, :].rearrange("p a b -> p (a b)"), g * S + t * P)
                          for g in range(A_KV) for t in range(TT)])
                if k == 2:
                    pe.wait_ge(first_in, 16 * 5)
                    pe.transpose(MIX[:, 0:P], vec_rows[:, :], ident[:, :])
                    n_rms = (B_QR + B_KVR) // P
                    pe.transpose(MIX[:, P:P + n_rms], rms_rows[:, :], ident[0:n_rms, 0:n_rms]).then_inc(cols_made, 1)
            products(xT_high, xT_low, KT, 1, gap=gap)

            def gap(k):
                if k in (1, 2):
                    if k == 1:
                        pe.wait_ge(acc_read[1], sets[1].now() * TT)
                    turn_rows(nat, 2 * (k - 1), 2)
                if k >= 3:
                    if k == 3:
                        pe.wait_ge(half_set, 1)
                    slot(k - 3, 0, A_HEADS)
            products(xT_high, xT_low, KT, 0, gap=gap)

            def gap(k):
                slot(5 + k, 0, A_HEADS)
                if k in (1, 2):
                    if k == 1:
                        pe.wait_ge(acc_read[0], sets[0].now() * TT)
                    turn_rows(nat, 2 * (k - 1), 2)
            products(xT_high, xT_low, KT, 1, EVEN_IN - CKV0, gap)

            def gap(k):
                if k < 6:
                    slot(13 + k, 0, A_HEADS)
                if k == 3:
                    pe.wait_ge(acc_read[1], sets[1].now() * TT)
                    turn_rows(nat, 0, 2)
            products(xT_high, xT_low, KT, 0, gap=gap)

            def late(t):
                if t - HEADS_AT in range(B_HEADS + LAG):
                    slot(t - HEADS_AT, A_HEADS, B_HEADS)
                rows = roped[:, :, :, :].rearrange("p t a b -> p t (a b)")
                if t == 1:
                    pe.wait_ge(rope_done, 1)
                    turn([(rows[:, u, :], u * P) for u in range(TT)])
                if t - 2 in range(PAIRS):
                    pe.wait_ge(acc_read[(t - 1) % 2], sets[(t - 1) % 2].now() * TT)
                    turn([(kbn[:, u, j, :], j * S + u * P) for j in range(2) for u in range(TT)])
                if t in (2, 3):
                    if t == 2:
                        pe.wait_ge(acc_read[0], TT * 3)
                    turn_rows(nat, 2 * (t - 2), 2)
                p, odd = (t - UQ_AT - 3) // 2, (t - UQ_AT - 3) % 2
                if p in range(PAIRS) and not odd:
                    pe.wait_ge(acc_read[(p + 1) % 2], TT * (5 + (p + 1) // 2))
                    turn([(qn[:, u, j, 0:B_NOPE], j * S + u * P) for j in range(2) for u in range(TT)])
                if p in range(PAIRS) and odd:
                    pe.wait_ge(rope_done, p + 2)
                    turn([(rows[:, u, :], u * P) for u in range(TT)])

            pe.wait_ge(keys_dup, 1)
            for p in range(PAIRS):
                if p == 0:
                    pe.wait_ge(work_cut, KT // 2 + 1)
                products(ckvT_high, ckvT_low, B_KVR // P, (p + 1) % 2, gap=lambda k: late(p))

            def latent_gap(k, p):
                late(UQ_AT + 2 * p + k)
                if p == 0 and k == 0:
                    pe.wait_ge(work_cut, KT // 2 + 3)
            for p in range(PAIRS):
                products(cqT_high, cqT_low, B_QR // P, (p + 1) % 2, UQW, lambda k: latent_gap(k, p))

            def projection(outputs, flip, beside):
                for s in range(D // N):
                    def gap(k):
                        if s == 0:
                            beside(k)
                            pe.wait_ge(mix_read, outputs + 2 * (k + 1))
                    products(mixT_high, mixT_low, KT, (s + flip) % 2, gap=gap, halves=True)

            def swiglu(layer, chunks, cut_before):
                def strips(before):
                    def gap(k):
                        if k in (1, 2):
                            if k == 1:
                                pe.wait_ge(acc_read[1], sets[1].now() * TT)
                            turn_rows(work, 2 * (k - 1), 2, bank=aux[k - 1], banks=2)
                    products(xT_high, xT_low, KT, 0, gap=gap if before else turning(chunks, cut_before))
                    products(xT_high, xT_low, KT, 1)

                strips(False)
                with repeated(pe, tallies, 1, FSTRIPS, units=2 * HALF_UNITS, set0=1, set1=1, turns=2):
                    strips(True)
                pe.wait_ge(acc_read[1], sets[1].now() * TT)
                for b in range(2):
                    turn_rows(work, 2 * b, 2, bank=aux[b], banks=2)
                pe.wait_ge(turn_read, turns.now())
                if layer == DEPTH - 1:
                    for s in range(D // N):
                        products(hid_high, hid_low, FT, s % 2, halves=True)
                else:
                    with repeated(pe, tallies, 0, D // N // 2, units=2 * DOWN_UNITS, set0=1, set1=1):
                        for s in range(2):
                            products(hid_high, hid_low, FT, s, halves=True)

            projection(0, 1, lambda k: late(OUT_AT + k))
            swiglu(0, 0, KT // 2 + 3)

            def odd_slot(s, i):
                n0 = HEADS_EVEN + i * GH
                if s - 2 in range(GH):
                    turn_probs(n0 + (s - 2), s % 2, probs)
                if s < GH:
                    n, par = n0 + s, s % 2
                    pe.wait_ge(scores_read, n)
                    pe.wait_ge(decay_ready, i * GH + (s + 1))
                    if s == 0:
                        pe.wait_ge(ones_ready, 1)
                    if s == 0:
                        pe.wait_ge(turn_read, turns.now())
                    late, ones = ones_late[:, P:2 * P], ones_late[:, :]
                    for m in range(2):
                        pe.matmul(SCORES[:, 0:P], decay[:, par, m, 0, :], late, start=(m == 0), stop=False)
                    pe.matmul(SCORES[:, 0:P], qTc[:, s, 0:P], kTc[:, s, 0:P], start=False, stop=True)
                    for m in range(2):
                        pe.matmul(SCORES[:, P:3 * P], decay[:, par, m, 2, :], ones, start=(m == 0), stop=False)
                        pe.matmul(SCORES[:, P:2 * P], decay[:, par, m, 1, :], late, start=False, stop=False)
                    pe.matmul(SCORES[:, P:3 * P], qTc[:, s, P:S], kTc[:, s, :], start=False, stop=True).then_inc(scores_made, 1)
                if s - LAG in range(GH):
                    j = s - LAG
                    if j == 0:
                        pe.wait_ge(acc_read[0], sets[0].now() * TT)
                    mix(n0 + j, j % 2, probsT, [vc[:, t, j * C_DIM:(j + 1) * C_DIM] for t in range(TT)],
                        m=MIX_EVEN + i * GH + j)

            def gate_products():
                pe.wait_ge(gate_cut, 1)
                for t in range(TT):
                    for k in range(KT):
                        for n, (a, b) in enumerate(((xT_high, gate_high), (xT_high, gate_low), (xT_low, gate_high))):
                            mm = pe.matmul(MIX[:, t * C_HEADS:(t + 1) * C_HEADS], a[:, k, t * P:(t + 1) * P], b[:, k, :],
                                           start=(k == 0 and n == 0), stop=(k == KT - 1 and n == 2))
                mm.then_inc(gates_made, 1)

            def group(i, first):
                def gap(k):
                    if k % 2 == 1:
                        odd_slot(k // 2, i - 1)
                products(xT_high, xT_low, KT, 0, gap=turning(D // N, KT + 3) if first else gap)

                def gap(k):
                    if first and k == 6:
                        gate_products()
                    if not first and k in (1, 3, 5):
                        odd_slot(4 + k // 2, i - 1)
                    if k in (2, 4):
                        if k == 2:
                            pe.wait_ge(acc_read[0], sets[0].now() * TT)
                        turn_rows(nat, k - 2, 2)
                products(xT_high, xT_low, KT, 1, gap=gap)

                def gap(k):
                    if k in (2, 4):
                        if k == 2:
                            pe.wait_ge(acc_read[1], sets[1].now() * TT)
                        turn_rows(nat, k - 2, 2)
                products(xT_high, xT_low, KT, 0, gap=gap)

            group(0, True)
            with repeated(pe, tallies, 1, GROUPS, units=3 * HALF_UNITS, set0=2, set1=1, turns=4) as i:
                group(i, False)

            def beside(k):
                if k < GH + LAG:
                    odd_slot(k, GROUPS - 1)
            projection(MIX_EVEN, 0, beside)
            swiglu(1, 2 * (D // N), 3 * KT // 2 + 3)

        @block.scalar
        def _(act):
            units, turns, z = Tally(), Tally(), Tally()
            seen = [Tally() for _ in range(SLOTS)]
            tallies = {"units": units, "turns": turns, "z": z} | {f"seen{s}": t for s, t in enumerate(seen)}
            SEEN = {f"seen{s}": 1 for s in range(SLOTS)}

            def round_ahead(more=AHEAD):
                if units.value + more >= UNITS:
                    return
                load, half = PLAN.get(units, "load", more), PLAN.get(units, "half", more)
                slot, width = PLAN.get(units, "slot", more), PLAN.get(units, "width", more)
                if half == 0:
                    seen[load].tick()
                    act.wait_ge(landed[load], seen[load].now() * 16)
                back = PLAN.nearest(units, "back", more)
                if back is not None:
                    act.wait_ge(multiplied, units.now(more + 1 - back))
                act.copy(w_high[:, slot, :, 0:width], raw[:, load, 2 * half:2 * half + 2, 0:width]).then_inc(rounded, 1)

            def unit():
                round_ahead()
                units.tick()

            def strip_done(k):
                act.wait_ge(multiplied, units.now(-k))

            def turn_read_to(out_ap, bank=TURN, width=N, dims=None):
                act.wait_ge(turned, turns.now(1))
                src = bank[:, 0:width]
                if dims:
                    src = src.rearrange("p (a b) -> p a b", a=dims)
                act.copy(out_ap, src).then_inc(turn_read, 1)
                turns.tick()

            def turn_to_work(bank, gain=None, bias=None):
                act.wait_ge(turned, turns.now(1))
                if z.value >= 2:
                    act.wait_ge(work_cut, z.now(-1))
                to = work[:, z.value % 2, :]
                if gain is None:
                    op = act.copy(to, bank[:, :])
                else:
                    for r in range(2):
                        part = slice(r * S, (r + 1) * S)
                        op = act.activation(to[:, part], bank[:, part], ACT.Identity, scale=gain[:, r:r + 1],
                                            bias=bias[:, r:r + 1] if bias is not None else 0.0)
                op.then_inc(turn_read, 1)
                turns.tick()
                z.tick()

            def turning(k, norm, lead=3):
                for b in range(lead) if k < 0 else range(k + lead - 1, min(k + lead, KT // 2)) if k else ():
                    if norm is None:
                        turn_to_work(aux[b % 4])
                    else:
                        at, bias_at = norm * KT + 2 * b, (2 * DEPTH + norm) * KT + 2 * b
                        turn_to_work(aux[b % 4], ln_cols[:, at:at + 2], ln_cols[:, bias_at:bias_at + 2])

            def exp_rows(n, parity, src, sink):
                act.wait_ge(maxed, n + 1)
                for t, (a, b) in enumerate(((0 if sink else 1, P + 1), (P + 1, 3 * P + (2 if sink else 1)))):
                    op = act.activation(src[:, parity, a:b], src[:, parity, a:b], ACT.Exp,
                                        bias=row_max[:, parity, t:t + 1], accum_out=row_sum[:, parity, t:t + 1])
                op.then_inc(exped, 1)

            def probs_copy(n, parity, to, first=False):
                act.wait_ge(probs_turned, n + 1)
                if not first:
                    act.wait_ge(mixed, n - 1)
                act.copy(to[:, parity, :], PROBS[:, 0:3 * P]).then_inc(probsT_made, 1)

            def mix_round(n, to):
                act.wait_ge(mixed, n + 1)
                act.copy(to, MIX[:, 0:S]).then_inc(mix_rounded, 1)

            def slot(s, first, count):
                h = first + s
                if s < count:
                    exp_rows(h, h % 2, probs, h < A_HEADS)
                if s - 2 in range(count):
                    probs_copy(h - 2, h % 2, probsT, first=(h - 2 < 2))
                h -= LAG
                if s - LAG in range(count) and (h >= A_HEADS or h % 2 == 1):
                    mix_round(h, mixT_high[:, MIX_A + h - A_HEADS if h >= A_HEADS else h // 2, :])

            def rms_squares(s, width):
                for t, spare in enumerate((kbn, qn)):
                    op = act.activation(spare[:, :, :, :].rearrange("p a b c -> p (a b c)")[:, 0:width],
                                        acc[s][t][:, 0:width], ACT.Square, accum_out=rms_sum[:, t:t + 1])
                op.then_inc(squares, 1)

            turning(-1, None, 2)
            for b in range(AHEAD):
                round_ahead(b)
            for k in range(HALF_UNITS):
                unit()
                turning(k, None, 2)
            for k in range(HALF_UNITS):
                unit()
                if k == 0:
                    strip_done(1)
                    for t in range(TT):
                        for dup in range(2):
                            act.copy(kan[:, t, :, dup, :], acc[0][t][:, 0:P].rearrange("p (g d) -> p g d", g=A_KV))
                        act.copy(va[:, t, :], acc[0][t][:, P:2 * P]).then_inc(acc_read[0], 1)
                if k == 1:
                    turn_read_to(kTa[:, :, :], dims=A_KV)
                if k == 2:
                    act.wait_ge(cols_made, 1)
                    act.copy(ln_cols[:, :], MIX[:, 0:P])
                    act.copy(rms_cols[:, :], MIX[:, P:P + (B_QR + B_KVR) // P]).then_inc(half_set, 1)
            act.wait_ge(half_set, 1)
            for k in range(HALF_UNITS):
                unit()
                if k == 0:
                    strip_done(1)
                    for t in range(TT):
                        act.mul(nat[:, t, :], acc[1][t][:, :], A_DIM ** -0.5).then_inc(acc_read[1], 1)
                if k in (1, 2):
                    turn_read_to(qTa[:, 2 * (k - 1):2 * k, :], dims=2)
                if k >= 3:
                    slot(k - 3, 0, A_HEADS)
            for k in range(HALF_UNITS):
                unit()
                if k == 0:
                    strip_done(1)
                    for t in range(TT):
                        act.mul(nat[:, t, :], acc[0][t][:, :], A_DIM ** -0.5).then_inc(acc_read[0], 1)
                slot(5 + k, 0, A_HEADS)
                if k in (1, 2):
                    turn_read_to(qTa[:, 2 + 2 * k:4 + 2 * k, :], dims=2)
            for k in range(HALF_UNITS):
                unit()
                if k == 0:
                    strip_done(1)
                    rms_squares(1, B_KVR)
                    for t in range(TT):
                        for dup in range(2):
                            op = act.copy(krn[:, t, dup, :], acc[1][t][:, B_KVR:B_KVR + B_ROPE])
                    op.then_inc(keys_dup, 1)
                if k < 6:
                    slot(13 + k, 0, A_HEADS)
                if k == 3:
                    turn_to_work(TURN, rms_cols[:, B_QR // P:(B_QR + B_KVR) // P])

            def late(t):
                if t - HEADS_AT in range(B_HEADS + LAG):
                    slot(t - HEADS_AT, A_HEADS, B_HEADS)
                if t == 0:
                    strip_done(1)
                    act.wait_ge(acc_read[1], TT * 2)
                    rms_squares(0, B_QR)
                if t == 1:
                    turn_read_to(kTr[:, :], width=S)
                if t - 2 in range(PAIRS):
                    turn_read_to(kTn[:, 2 * (t - 2):2 * (t - 1), :], dims=2)
                if t in (2, 3):
                    turn_to_work(TURN, rms_cols[:, 2 * (t - 2):2 * (t - 1)])
                p, odd = (t - UQ_AT - 3) // 2, (t - UQ_AT - 3) % 2
                if p in range(PAIRS) and not odd:
                    turn_read_to(qTn[:, 2 * p:2 * p + 2, :], dims=2)
                if p in range(PAIRS) and odd:
                    turn_read_to(qTr[:, p, :], width=S)
                if t - 1 in range(PAIRS):
                    p = t - 1
                    strip_done(1)
                    if p == 0:
                        act.wait_ge(squares, 2)
                    for u in range(TT):
                        both_kv = acc[(p + 1) % 2][u][:, :].rearrange("p (j c) -> p j c", j=2)
                        act.copy(kbn[:, u, :, :], both_kv[:, :, 0:B_NOPE])
                        act.copy(vb[:, u, 2 * p:2 * p + 2, :], both_kv[:, :, B_NOPE:]).then_inc(acc_read[(p + 1) % 2], 1)
                p, odd = (t - UQ_AT - 2) // 2, (t - UQ_AT - 2) % 2
                if p in range(PAIRS) and not odd:
                    strip_done(1)
                    if p:
                        act.wait_ge(rope_done, p + 1)
                    for u in range(TT):
                        act.mul(qn[:, u, :, :], acc[(p + 1) % 2][u][:, 0:UQW].rearrange("p (j c) -> p j c", j=2),
                                (B_NOPE + B_ROPE) ** -0.5).then_inc(acc_read[(p + 1) % 2], 1)

            for t in range(OUT_AT):
                unit()
                late(t)

            def projection(beside):
                for s in range(D // N):
                    for k in range(HALF_UNITS):
                        unit()
                        if s == 0:
                            beside(k)

            def swiglu(layer):
                def hidden_round(i):
                    for b in range(2):
                        act.wait_ge(turned, turns.now(1))
                        act.copy(hid_high[:, bass.ds(i * 4 + 2 * b, 2), :] if not isinstance(i, int)
                                 else hid_high[:, 4 * i + 2 * b:4 * i + 2 * b + 2, :],
                                 aux[b][:, :].rearrange("p (a b) -> p a b", a=2)).then_inc(hid_rounded, 1)
                        turns.tick()

                def strips(i, before):
                    if not before:
                        turning(-1, 2 * layer)
                    for k in range(HALF_UNITS):
                        unit()
                        if not before:
                            turning(k, 2 * layer)
                        if before and k == 1:
                            hidden_round(i - 1)
                    for k in range(HALF_UNITS):
                        unit()
                        if k == 0:
                            strip_done(1)
                            act.wait_ge(turned, turns.now())
                            for t in range(TT):
                                act.activation(work[:, t, :], acc[0][t][:, :], ACT.Silu).then_inc(acc_read[0], 1)

                strips(0, False)
                act.wait_ge(affine, 2 * layer + 1)
                with repeated(act, tallies, 1, FSTRIPS, units=2 * HALF_UNITS, turns=2,
                              **{k: 2 * v for k, v in SEEN.items()}) as i:
                    strips(i, True)
                hidden_round(FSTRIPS - 1)
                if layer == DEPTH - 1:
                    for k in range(D // N * DOWN_UNITS):
                        unit()
                else:
                    with repeated(act, tallies, 0, D // N // 2, units=2 * DOWN_UNITS, seen0=6, seen1=6, seen2=6, seen3=4):
                        for k in range(2 * DOWN_UNITS):
                            unit()

            projection(lambda k: late(OUT_AT + k))
            swiglu(0)

            def odd_slot(s, i):
                n0 = HEADS_EVEN + i * GH
                if s < GH:
                    exp_rows(n0 + s, s % 2, probs, False)
                if s - 2 in range(GH):
                    probs_copy(n0 + (s - 2), s % 2, probsT)
                if s - LAG in range(GH):
                    m = i * GH + (s - LAG)
                    to = mixT_high[:, m, :] if isinstance(i, int) else \
                        mixT_high[:, bass.ds(m, 1), :].rearrange("p a b -> p (a b)")
                    mix_round(n0 + (s - LAG), to)

            def values_out():
                act.copy(vc[:, 0, :], acc[0][0][:, :]).then_inc(acc_read[0], 1)

            def group(i, first):
                if first:
                    turning(-1, 1)
                for k in range(HALF_UNITS):
                    unit()
                    if first:
                        turning(k, 1)
                    if not first and k == 0:
                        strip_done(1)
                        values_out()
                    if not first and k % 2 == 1:
                        odd_slot(k // 2, i - 1)
                for k in range(HALF_UNITS):
                    unit()
                    if k == 0:
                        strip_done(1)
                        act.wait_ge(turned, turns.now())
                        for t in range(TT):
                            act.mul(nat[:, t, :], acc[0][t][:, :], C_DIM ** -0.5).then_inc(acc_read[0], 1)
                    if not first and k in (1, 3, 5):
                        odd_slot(4 + k // 2, i - 1)
                    if k in (2, 4):
                        turn_read_to(qTc[:, k - 2:k, :], dims=2)
                    if first and k == 4:
                        act.wait_ge(odd_in, 16 * 4)
                        act.copy(gate_high[:, :, :], gate_raw[:, :, :]).then_inc(gate_rounded, 1)
                    if first and k == 6:
                        log_sigmoid()
                for k in range(HALF_UNITS):
                    unit()
                    if k == 0:
                        strip_done(1)
                        act.wait_ge(turned, turns.now())
                        for t in range(TT):
                            act.copy(nat[:, t, :], acc[1][t][:, :]).then_inc(acc_read[1], 1)
                    if k in (2, 4):
                        turn_read_to(kTc[:, k - 2:k, :], dims=2)

            def log_sigmoid():
                act.wait_ge(gate_bias, 1)
                act.activation(gate_tmp[:, 1, :, :], gate_tmp[:, 0, :, :], ACT.Abs).then_inc(gate_abs, 1)
                act.wait_ge(gate_abs, 1)
                act.activation(gate_tmp[:, 2, :, :], gate_tmp[:, 1, :, :], ACT.Exp, scale=-1.0).then_inc(gate_abs, 1)
                act.wait_ge(gate_abs, 2)
                act.activation(gate_tmp[:, 3, :, :], gate_tmp[:, 2, :, :], ACT.Ln, bias=1.0).then_inc(gate_ln, 1)

            group(0, True)
            with repeated(act, tallies, 1, GROUPS, units=3 * HALF_UNITS, turns=4,
                          **{k: 3 * v for k, v in SEEN.items()}) as i:
                group(i, False)

            def beside(k):
                if k == 0:
                    strip_done(1)
                    values_out()
                if k < GH + LAG:
                    odd_slot(k, GROUPS - 1)
            projection(beside)
            swiglu(1)
            act.wait_ge(end_shift, 1)
            for c in range(D // N):
                cols = slice(c * N, (c + 1) * N)
                act.activation(x[:, 1, cols], x[:, 1, cols], ACT.Identity, scale=rstd[:, 1:2],
                               bias=minus_mean[:, 0:1]).then_inc(end_scaled, 1)

        @block.vector
        def _(dve):
            units, turns, z, own, sums = Tally(), Tally(), Tally(), Tally(), Tally()
            tallies = {"units": units, "turns": turns, "z": z, "own": own, "sums": sums}

            def cut_ahead(more=AHEAD):
                if units.value + more >= UNITS:
                    return
                load, half = PLAN.get(units, "load", more), PLAN.get(units, "half", more)
                slot, width = PLAN.get(units, "slot", more), PLAN.get(units, "width", more)
                dve.wait_ge(rounded, units.now(more + 1))
                dve.tensor_tensor(w_low[:, slot, :, 0:width], raw[:, load, 2 * half:2 * half + 2, 0:width],
                                  w_high[:, slot, :, 0:width].bitcast(F32), ALU.subtract).then_inc(cut, 1)

            def unit():
                cut_ahead()
                units.tick()

            def strip_done(k):
                dve.wait_ge(multiplied, units.now(-k))

            def result(op):
                op.then_inc(vector_self, 1)
                own.tick()
                dve.wait_ge(vector_self, own.now())

            def work_to(high, low):
                turns.tick()
                src = work[:, z.value % 2, :].rearrange("p (a b) -> p a b", a=2)
                dve.wait_ge(turn_read, turns.now())
                dve.tensor_copy(high, src).then_inc(work_high, 1)
                dve.wait_ge(work_high, z.now(1))
                dve.tensor_tensor(low, src, high.bitcast(F32), ALU.subtract).then_inc(work_cut, 1)
                z.tick()

            def residual(s, cols, at, k):
                for t in range(TT):
                    if t == 0:
                        halves.tick()
                        dve.wait_ge(half_multiplied, halves.now())
                    else:
                        dve.wait_ge(multiplied, units.now(-k))
                    dve.scalar_tensor_tensor(out=x[:, t, cols], in0=x[:, t, cols], scalar=ALPHA, in1=acc[s][t][:, :],
                                             op0=ALU.mult, op1=ALU.add).then_inc(acc_read[s], 1)
                    sums_of[s].tick()
                    dve.wait_ge(acc_read[s], sums_of[s].now())
                    dve.bn_stats(stats[:, t, at, :] if isinstance(at, int) else
                                 stats[:, t, bass.ds(at, 1), :].rearrange("p a b -> p (a b)"), x[:, t, cols])\
                       .then_inc(vector_self, 1)
                    own.tick()

            def projection(count_units, flip=0, beside=None):
                for s in range(D // N):
                    for k in range(count_units):
                        unit()
                        if s == 0 and beside:
                            beside(k)
                        if s and k == 0:
                            residual((s - 1 + flip) % 2, slice((s - 1) * N, s * N), s - 1, 1)
                residual((s + flip) % 2, slice(s * N, D), s, 0)

            def projection_pairs(count_units):
                with repeated(dve, tallies, 0, D // N // 2, units=2 * count_units, own=2 * TT, halves=2,
                              acc0=TT, acc1=TT) as i:
                    for s in range(2):
                        for k in range(count_units):
                            unit()
                            if s == 1 and k == 0:
                                residual(0, bass.ds(i * (2 * N), N), 2 * i, 1)
                    residual(1, bass.ds(i * (2 * N) + N, N), 2 * i + 1, 0)

            def moments_of(k):
                dve.wait_ge(vector_self, own.now())
                for t in range(TT):
                    op = dve.bn_aggr(moments[:, t, :], stats[:, t, :, :].rearrange("p a b -> p (a b)"))
                result(op)
                dve.tensor_scalar(var_eps[:, :], moments[:, :, 1], LN_EPS, None, ALU.add).then_inc(var_ready, 1)
                dve.wait_ge(rstd_ready, 3 + k)

            def normalise_chunk(c):
                cols = slice(c * N, (c + 1) * N)
                for t in range(TT):
                    op = dve.tensor_scalar(x[:, t, cols], x[:, t, cols], moments[:, t, 0:1], rstd[:, t:t + 1],
                                           ALU.subtract, ALU.mult)
                op.then_inc(normed, 1)

            def turning(k, norm, lead=3):
                if k < 0 and norm is not None:
                    moments_of(norm)
                    normalise_chunk(0)
                    normalise_chunk(1)
                for b in range(lead) if k < 0 else range(k + lead - 1, min(k + lead, KT // 2)) if k else ():
                    work_to(xT_high[:, 2 * b:2 * b + 2, :], xT_low[:, 2 * b:2 * b + 2, :])
                if k < 0 and norm is not None:
                    normalise_chunk(2)
                    normalise_chunk(3)

            def read_scores(n, parity, to, bias, slope=None, first=False):
                dve.wait_ge(scores_made, n + 1)
                if not first:
                    dve.wait_ge(probs_turned, n - 1)
                if slope is not None:
                    op = dve.scalar_tensor_tensor(out=to[:, parity, 1:3 * P + 1], in0=bias, scalar=slope,
                                                  in1=SCORES[:, 0:3 * P], op0=ALU.mult, op1=ALU.add)
                else:
                    op = dve.tensor_tensor(to[:, parity, 1:3 * P + 1], SCORES[:, 0:3 * P], bias, ALU.add)
                op.then_inc(scores_read, 1)
                dve.wait_ge(scores_read, n + 1)
                sink = slope is not None
                if sink:
                    dve.wait_ge(sink_set, n + 1)
                for t, (a, b) in enumerate(((0 if sink else 1, P + 1), (P + 1, 3 * P + (2 if sink else 1)))):
                    op = dve.tensor_reduce(row_max[:, parity, t:t + 1], to[:, parity, a:b], AX_X, ALU.max, negate=True)
                op.then_inc(maxed, 1)

            def normalise(n, parity, to):
                dve.wait_ge(exped, n + 1)
                dve.reciprocal(row_inv[:, parity, :], row_sum[:, parity, :]).then_inc(summed, 1)
                dve.wait_ge(summed, n + 1)
                for t, (a, b) in enumerate(((1, P + 1), (P + 1, 3 * P + 1))):
                    op = dve.tensor_scalar(to[:, parity, a:b], to[:, parity, a:b], row_inv[:, parity, t:t + 1], None, ALU.mult)
                op.then_inc(probs_made, 1)

            def mix_low(m, high, low):
                dve.wait_ge(mix_rounded, m + 1)
                dve.tensor_tensor(low, MIX[:, 0:S], high.bitcast(F32), ALU.subtract).then_inc(mix_read, 1)

            sums_of = [Tally(), Tally()]
            tallies["acc0"], tallies["acc1"] = sums_of

            halves = Tally()
            tallies["halves"] = halves

            def rms(s, width, round_no):
                dve.wait_ge(squares, round_no)
                dve.tensor_scalar(var_eps[:, :], rms_sum[:, :], 1.0 / width, RMS_EPS, ALU.mult, ALU.add).then_inc(var_ready, 1)
                dve.wait_ge(turned, turns.now())
                dve.wait_ge(rstd_ready, round_no)
                if round_no == 1:
                    dve.wait_ge(keys_dup, 1)
                for t in range(TT):
                    dve.tensor_scalar(nat[:, t, 0:width], acc[s][t][:, 0:width], rstd[:, t:t + 1], None,
                                      ALU.mult).then_inc(acc_read[s], 1)

            def slot(s, first, count):
                h = first + s
                if s < count:
                    if h < A_HEADS:
                        read_scores(h, h % 2, probs, dist_a[:, :], slopes[:, h:h + 1], first=(h < 2))
                    else:
                        read_scores(h, h % 2, probs, mask_b[:, :])
                if s - 1 in range(count):
                    normalise(h - 1, (h - 1) % 2, probs)
                h -= LAG
                if s - LAG in range(count) and (h >= A_HEADS or h % 2 == 1):
                    m = MIX_A + h - A_HEADS if h >= A_HEADS else h // 2
                    mix_low(m, mixT_high[:, m, :], mixT_low[:, m, :])

            turning(-1, None, 2)
            for b in range(AHEAD):
                cut_ahead(b)
            for k in range(HALF_UNITS):
                unit()
                turning(k, None, 2)
            for k in range(HALF_UNITS):
                unit()
                if k == 1:
                    turns.tick()
            dve.wait_ge(even_in, 16 * 6)
            for k in range(HALF_UNITS):
                unit()
                if k in (1, 2):
                    turns.tick()
                if k >= 3:
                    slot(k - 3, 0, A_HEADS)
            for k in range(HALF_UNITS):
                unit()
                slot(5 + k, 0, A_HEADS)
                if k in (1, 2):
                    turns.tick()
            for k in range(HALF_UNITS):
                unit()
                if k < 6:
                    slot(13 + k, 0, A_HEADS)
                if k == 0:
                    rms(1, B_KVR, 1)
                if k == 3:
                    work_to(ckvT_high[:, :, :], ckvT_low[:, :, :])

            def late(t):
                if t - HEADS_AT in range(B_HEADS + LAG):
                    slot(t - HEADS_AT, A_HEADS, B_HEADS)
                if t == 0:
                    rms(0, B_QR, 2)
                if t == 1:
                    turns.tick()
                if t - 2 in range(PAIRS):
                    turns.tick()
                if t in (2, 3):
                    b = 2 * (t - 2)
                    work_to(cqT_high[:, b:b + 2, :], cqT_low[:, b:b + 2, :])
                if t - UQ_AT - 3 in range(2 * PAIRS):
                    turns.tick()

            for t in range(OUT_AT):
                unit()
                late(t)
            sums_of[0].value = TT * (3 + PAIRS)
            sums_of[1].value = TT * (2 + PAIRS)

            def swiglu(layer):
                def hidden_low(i):
                    for b in range(2):
                        dve.wait_ge(hid_rounded, hids.now(1))
                        at = slice(4 * i + 2 * b, 4 * i + 2 * b + 2) if isinstance(i, int) else bass.ds(i * 4 + 2 * b, 2)
                        dve.tensor_tensor(hid_low[:, at, :], aux[b][:, :].rearrange("p (a b) -> p a b", a=2),
                                          hid_high[:, at, :].bitcast(F32), ALU.subtract).then_inc(turn_read, 1)
                        hids.tick()
                        turns.tick()

                def gate_up(k):
                    dve.wait_ge(acc_read[0], sums_of[0].now(TT))
                    strip_done(k)
                    for t in range(TT):
                        dve.tensor_tensor(work[:, t, :], acc[1][t][:, :], work[:, t, :], ALU.mult).then_inc(acc_read[1], 1)
                    sums_of[0].tick(TT)
                    sums_of[1].tick(TT)

                def strips(i, before):
                    if not before:
                        turning(-1, 2 * layer)
                    for k in range(HALF_UNITS):
                        unit()
                        if not before:
                            turning(k, 2 * layer)
                        if before and k == 0:
                            gate_up(1)
                        if before and k == 1:
                            hidden_low(i - 1)
                    for k in range(HALF_UNITS):
                        unit()
                strips(0, False)
                dve.wait_ge(affine, 2 * layer + 1)
                with repeated(dve, tallies, 1, FSTRIPS, units=2 * HALF_UNITS, turns=2, hids=2, acc0=TT, acc1=TT) as i:
                    strips(i, True)
                gate_up(0)
                hidden_low(FSTRIPS - 1)
                if layer == DEPTH - 1:
                    projection(DOWN_UNITS)
                else:
                    projection_pairs(DOWN_UNITS)

            hids = Tally()
            tallies["hids"] = hids
            projection(HALF_UNITS, 1, lambda k: late(OUT_AT + k))
            swiglu(0)

            def odd_slot(s, i):
                n0 = HEADS_EVEN + i * GH
                if s < GH:
                    read_scores(n0 + s, s % 2, probs, mask_c[:, :])
                if s - 1 in range(GH):
                    normalise(n0 + (s - 1), (s - 1) % 2, probs)
                if s - LAG in range(GH):
                    m = i * GH + (s - LAG)
                    high, low = (w[:, m, :] if isinstance(i, int) else
                                 w[:, bass.ds(m, 1), :].rearrange("p a b -> p (a b)") for w in (mixT_high, mixT_low))
                    mix_low(m + MIX_EVEN, high, low)

            def values_out():
                dve.tensor_copy(vc[:, 1, :], acc[0][1][:, :]).then_inc(acc_read[0], 1)

            def group(i, first):
                if first:
                    turning(-1, 1)
                for k in range(HALF_UNITS):
                    unit()
                    if first:
                        turning(k, 1)
                    if not first and k == 0:
                        strip_done(1)
                        values_out()
                    if not first and k % 2 == 1:
                        odd_slot(k // 2, i - 1)
                for k in range(HALF_UNITS):
                    unit()
                    if not first and k in (1, 3, 5):
                        odd_slot(4 + k // 2, i - 1)
                    if first and k == 4:
                        dve.wait_ge(gate_rounded, 1)
                        dve.tensor_tensor(gate_low[:, :, :], gate_raw[:, :, :], gate_high[:, :, :].bitcast(F32),
                                          ALU.subtract).then_inc(gate_cut, 1)
                        dve.tensor_copy(ones_late[:, :], tri[:, P:3 * P]).then_inc(ones_ready, 1)
                    if first and k == 6:
                        forget_gates()
                for k in range(HALF_UNITS):
                    unit()

            def forget_gates():
                dve.wait_ge(gates_made, 1)
                sums_ap = MIX[:, 0:TT * C_HEADS].rearrange("p (t h) -> p t h", t=TT)
                for t in range(TT):
                    op = dve.tensor_tensor(gate_tmp[:, 0, t, :], sums_ap[:, t, :], f_bias[:, :], ALU.add)
                op.then_inc(gate_bias, 1)
                dve.wait_ge(gate_bias, 1)
                result(dve.tensor_scalar(log_f[:, :, :], gate_tmp[:, 0, :, :], 0.0, None, ALU.min))
                dve.wait_ge(gate_ln, 1)
                result(dve.tensor_tensor(log_f[:, :, :], log_f[:, :, :], gate_tmp[:, 3, :, :], ALU.subtract))
                result(dve.tensor_copy(log_f_high[:, :, :], log_f[:, :, :]))
                dve.tensor_tensor(log_f_low[:, :, :], log_f[:, :, :], log_f_high[:, :, :].bitcast(F32),
                                  ALU.subtract).then_inc(forget_ready, 1)

            group(0, True)
            with repeated(dve, tallies, 1, GROUPS, units=3 * HALF_UNITS) as i:
                group(i, False)
            turns.tick(4 * GROUPS)
            sums_of[0].tick(2 * TT * GROUPS)
            sums_of[1].tick(TT * GROUPS)
            dve.wait_ge(affine, 2)

            def beside(k):
                if k == 0:
                    strip_done(1)
                    values_out()
                if k < GH + LAG:
                    odd_slot(k, GROUPS - 1)
            projection(HALF_UNITS, 0, beside)
            swiglu(1)
            moments_of(3)
            dve.tensor_scalar(minus_mean[:, :], moments[:, 1, 0:1], rstd[:, 1:2], -1.0, ALU.mult, ALU.mult).then_inc(end_shift, 1)
            dve.wait_ge(rows_in, 32 * 4)
            for c in range(D // N):
                cols = slice(c * N, (c + 1) * N)
                result(dve.scalar_tensor_tensor(out=x[:, 0, cols], in0=x[:, 0, cols], scalar=moments[:, 0, 0:1],
                                                in1=ln_rows_end[:, 0, cols], op0=ALU.subtract, op1=ALU.mult))
                dve.scalar_tensor_tensor(out=x[:, 0, cols], in0=x[:, 0, cols], scalar=rstd[:, 0:1],
                                         in1=ln_rows_end[:, 1, cols], op0=ALU.mult, op1=ALU.add).then_inc(affine, 1)

        @block.gpsimd
        def _(pool):
            own = Tally()

            def result(op):
                op.then_inc(pool_self, 1)
                own.tick()
                pool.wait_ge(pool_self, own.now())

            def inverse_root(n):
                pool.wait_ge(var_ready, n)
                pool.tensor_tensor(rstd[:, :], var_eps[:, :], minus_half[:, :], ALU.pow).then_inc(rstd_ready, 1)

            def rotate(src, n):
                h = B_ROPE // 2
                x1, x2 = src[:, :, :, 0:h], src[:, :, :, h:B_ROPE]
                cos, sin = (c[:, :].rearrange("p (t j h) -> p t j h", t=TT, j=2) for c in (cos_t, sin_t))
                for k, (a, b) in enumerate(((x1, cos), (x2, sin), (x2, cos), (x1, sin))):
                    op = pool.tensor_tensor(rope_tmp[:, k, :, :, :], a, b, ALU.mult)
                result(op)
                pool.tensor_tensor(roped[:, :, :, 0:h], rope_tmp[:, 0, :, :, :], rope_tmp[:, 1, :, :, :], ALU.subtract)
                pool.tensor_tensor(roped[:, :, :, h:B_ROPE], rope_tmp[:, 2, :, :, :], rope_tmp[:, 3, :, :, :], ALU.add)\
                    .then_inc(rope_done, 1)

            def affine_rows(k, turned_before):
                pool.wait_ge(rows_in, 32 * (k + 1))
                pool.wait_ge(turned, turned_before)
                for t in range(TT):
                    op = pool.tensor_tensor(x[:, t, :], x[:, t, :], ln_rows[:, 0, :], ALU.mult)
                result(op)
                for t in range(TT):
                    op = pool.tensor_tensor(x[:, t, :], x[:, t, :], ln_rows[:, 1, :], ALU.add)
                op.then_inc(affine, 1)

            pool.memset(minus_half[:, :], -0.5).then_inc(pool_self, 1)
            own.tick()
            pool.wait_ge(pool_self, 1)
            def set_sink(s):
                if s >= 2:
                    pool.wait_ge(probs_turned, s - 1)
                pool.tensor_copy(probs[:, s % 2, 0:1], sinks[:, s:s + 1])
                pool.tensor_copy(probs[:, s % 2, 3 * P + 1:3 * P + 2], sinks[:, s:s + 1]).then_inc(sink_set, 1)

            pool.wait_ge(even_in, 16 * 6)
            for s in range(14):
                set_sink(s)
            inverse_root(1)
            set_sink(14)
            set_sink(15)
            pool.wait_ge(keys_dup, 1)
            rotate(krn, 0)
            inverse_root(2)
            KEYS_TURNED = KT // 2 + 1 + 2 + 2 + 1 + 1
            PAIR_TURNED = KEYS_TURNED + PAIRS + 2
            for p in range(PAIRS):
                pool.wait_ge(acc_read[(p + 1) % 2], TT * (5 + (p + 1) // 2))
                pool.wait_ge(turned, PAIR_TURNED + 2 * p if p else KEYS_TURNED)
                rotate(qn[:, :, :, B_NOPE:], p + 1)
            inverse_root(3)
            turns = PAIR_TURNED + 2 * PAIRS + KT // 2
            affine_rows(0, turns)
            inverse_root(4)
            turns += 2 * FSTRIPS + KT // 2
            affine_rows(1, turns)

            pool.wait_ge(forget_ready, 1)

            def decays(i):
                group = slice(GH * i, GH * (i + 1)) if isinstance(i, int) else bass.ds(i * GH, GH)
                pool.tensor_copy(group_f[:, 0, :, :], log_f_high[:, :, group].bitcast(F32))
                result(pool.tensor_copy(group_f[:, 1, :, :], log_f_low[:, :, group]))
                for j in range(GH):
                    pool.wait_ge(scores_made, HEADS_EVEN + i * GH + (j - 1))
                    for m in range(2):
                        pool.tensor_tensor(decay[:, j % 2, m, 0:2, :].rearrange("p a b -> p (a b)"), tri[:, 0:2 * P],
                                           group_f[:, m, 0, j:j + 1].to_broadcast([P, 2 * P]), ALU.mult)
                        op = pool.tensor_tensor(decay[:, j % 2, m, 2, :], tri[:, 0:P],
                                                group_f[:, m, 1, j:j + 1].to_broadcast([P, P]), ALU.mult)
                    op.then_inc(decay_ready, 1)
                pool.wait_ge(decay_ready, i * GH + GH)

            with repeated(pool, {"own": own}, 0, GROUPS, own=1) as i:
                decays(i)
            inverse_root(5)
            turns += 4 * GROUPS + KT // 2
            affine_rows(2, turns)
            inverse_root(6)
            pool.wait_ge(rows_in, 32 * 4)
            for c in range(D // N):
                cols = slice(c * N, (c + 1) * N)
                pool.wait_ge(end_scaled, c + 1)
                result(pool.tensor_tensor(x[:, 1, cols], x[:, 1, cols], ln_rows_end[:, 0, cols], ALU.mult))
                pool.tensor_tensor(x[:, 1, cols], x[:, 1, cols], ln_rows_end[:, 1, cols], ALU.add).then_inc(end_second, 1)


_INS = ["x", "even_w_in", "even_sinks", "even_q_norm", "even_w_uq", "even_kv_norm", "even_w_ukv", "even_w_out",
        "odd_w_in", "odd_forget_bias", "odd_w_out", "ffn_w_gate", "ffn_w_up", "ffn_w_down", "ln_gain", "ln_bias"]


def kernel(**inputs):
    import concourse.bacc as _bacc
    from concourse.bass_utils import run_bass_kernel_spmd as _run

    nc = _bacc.Bacc("TRN2", target_bir_lowering=False, num_devices=1)
    arrays = {f"in_{name}": np.ascontiguousarray(inputs[name]) for name in _INS}
    arrays["in_constants"] = constants()
    args = [nc.dram_tensor(n, a.shape, mybir.dt.from_np(a.dtype), kind="ExternalInput").ap() for n, a in arrays.items()]
    out = nc.dram_tensor("out_0", (1, S, D), F32, kind="ExternalOutput").ap()
    trunk(nc, *args, out)
    r = _run(nc, [arrays], core_ids=[0])
    return r.results[0]["out_0"]
```

```python
from contextlib import ExitStack, contextmanager

import numpy as np

import concourse.bass as bass
from concourse import mybir

F32 = mybir.dt.float32
F32R = mybir.dt.float32r
ALU = mybir.AluOpType
ACT = mybir.ActivationFunctionType
AX_X = mybir.AxisListType.X

P = 128
D = 2048
KT = D // P
S = 256
TT = S // P
N = 512
DEPTH = 2
D_FF = 5632
FT = D_FF // P
FSTRIPS = D_FF // N
ALPHA = (2 * DEPTH) ** 0.25
LN_EPS = 1e-5
RMS_EPS = 1e-6

A_HEADS, A_KV, A_DIM = 16, 2, 64
B_HEADS, B_NOPE, B_ROPE, B_V = 8, 128, 64, 128
B_QR, B_KVR = 512, 256
C_HEADS, C_DIM = 16, 128
CHUNK = 64
A_Q = A_HEADS * A_DIM
KA0 = A_Q
VA0 = KA0 + A_KV * A_DIM
CQ0 = VA0 + A_KV * A_DIM
CKV0 = CQ0 + B_QR
KR0 = CKV0 + B_KVR
EVEN_IN = KR0 + B_ROPE
C_HD = C_HEADS * C_DIM
ODD_IN = 3 * C_HD + C_HEADS
GROUPS = C_HD // N
GH = N // C_DIM
HEADS_EVEN = A_HEADS + B_HEADS
MIX_A = A_HEADS // 2
PAIRS = B_HEADS // 2
BIG = 1e30

SLOTS = 4
AHEAD = 3
LAG = 3
UQW = 2 * (B_NOPE + B_ROPE)

C_ID, C_U, C_ONE, C_G, C_MC, C_DA, C_MB, C_COS, C_SIN, C_SL = np.cumsum([0, P, P, P, P, 3 * P, 3 * P, 3 * P, P, P]).tolist()
C_END = C_SL + A_HEADS


def constants():
    c = np.zeros((P, C_END), np.float32)
    r = np.arange(P)
    c[:, C_ID:C_ID + P] = np.eye(P)
    c[:, C_U:C_U + P] = r[:, None] <= r[None, :]
    c[:, C_ONE:C_ONE + P] = 1
    c[:, C_G:C_G + P] = r[:, None] > r[None, :]
    pairs = [(0, 0), (1, 0), (1, 1)]
    for n, (tq, tk) in enumerate(pairs):
        q, k = tq * P + r[:, None], tk * P + r[None, :]
        cq, ck = q // CHUNK, k // CHUNK
        at = slice(n * P, (n + 1) * P)
        c[:, C_MC:C_DA][:, at] = np.where(k <= q, 0, -BIG)
        c[:, C_DA:C_MB][:, at] = np.where((ck <= cq) & (ck >= cq - 1), np.abs(q - k), BIG)
        c[:, C_MB:C_COS][:, at] = np.where(ck <= cq, 0, -BIG)
    inv = (10000.0 ** (-np.arange(0, B_ROPE, 2, dtype=np.float32) / np.float32(B_ROPE))).astype(np.float32)
    ang = np.arange(S, dtype=np.float32)[:, None] * inv[None, :]
    for at, f in ((C_COS, np.cos), (C_SIN, np.sin)):
        t = f(ang).astype(np.float32).reshape(TT, P, 1, B_ROPE // 2).transpose(1, 0, 2, 3)
        c[:, at:at + P] = np.broadcast_to(t, (P, TT, 2, B_ROPE // 2)).reshape(P, P)
    c[:, C_SL:C_END] = -np.exp2(-8.0 * (np.arange(A_HEADS, dtype=np.float32) + 1) / A_HEADS)
    return c


class Tally:

    def __init__(self):
        self.value, self.i, self.times = 0, None, 1

    def enter(self, i, first, times, per):
        self.i, self.first, self.times, self.per, self.start = i, first, times, per, self.value

    def leave(self):
        assert self.value == self.start + self.per, (self.value, self.start, self.per)
        self.value = self.start + self.per * self.times
        self.i, self.times, self.per = None, 1, 0

    def now(self, more=0):
        if self.i is None or not self.per:
            return self.value + more
        return self.i * self.per + (self.value - self.first * self.per + more)

    def rounds(self):
        return [self.value + m * self.per for m in range(self.times)] if self.i is not None else [self.value]

    def tick(self, n=1):
        self.value += n


@contextmanager
def repeated(engine, tallies, first, end, **per):
    with engine.Fori(first, end) as i:
        for name, t in tallies.items():
            t.enter(i, first, end - first, per.get(name, 0))
        yield i
    for t in tallies.values():
        t.leave()


class Plan:

    def __init__(self):
        self.units = []
        strips = [(KT, CQ0 - KA0), (KT, N), (KT, N), (KT, EVEN_IN - CKV0), (KT, N)]
        strips += [(B_KVR // P, N)] * PAIRS + [(B_QR // P, UQW)] * PAIRS
        ffn = [(KT, N)] * (2 * FSTRIPS) + [(FT, N)] * (D // N)
        strips += [(KT, N)] * (D // N) + ffn + [(KT, N)] * (3 * GROUPS + D // N) + ffn
        slot = load = 0
        last_in_slot, last_in_load, uses = {}, {}, [0] * SLOTS
        for kts, width in strips:
            for k in range(0, kts, 2):
                u = len(self.units)
                x = dict(slot=slot, back=u - last_in_slot[slot] if slot in last_in_slot else None,
                         width=width, half=k // 2 % 2, load=load)
                if k % 4 == 0:
                    x["load_back"] = u - last_in_load[load] if load in last_in_load else None
                    uses[load] += 1
                    x["uses"] = uses[load]
                self.units.append(x)
                last_in_slot[slot] = u
                last_in_load[load] = u
                slot = (slot + 1) % SLOTS
                if k % 4 == 2 or k + 2 >= kts:
                    load = (load + 1) % SLOTS

    def get(self, tally, key, more=0):
        found = [self.units[u + more][key] for u in tally.rounds()]
        assert len(set(found)) == 1, (key, found)
        return found[0]

    def nearest(self, tally, key, more=0):
        found = [self.units[u + more][key] for u in tally.rounds()]
        return min(x for x in found if x is not None) if any(x is not None for x in found) else None


PLAN = Plan()
UNITS = len(PLAN.units)


def trunk(nc, x_in, even_w_in, even_sinks, even_q_norm, even_w_uq, even_kv_norm, even_w_ukv, even_w_out,
          odd_w_in, odd_forget_bias, odd_w_out, ffn_w_gate, ffn_w_up, ffn_w_down, ln_gain, ln_bias, consts, out):
    ctx = ExitStack()
    with ctx:
        def sb(name, shape, dt=F32):
            return ctx.enter_context(nc.sbuf_tensor(name, shape, dt))

        def overlaid(*tensors):
            with ExitStack() as room:
                return [room.enter_context(nc.sbuf_tensor(*t)) for t in tensors]

        def sem(name):
            return ctx.enter_context(nc.semaphore(name))

        raw = sb("raw", [P, SLOTS, 4, N])
        w_high = sb("w_high", [P, SLOTS, 2, N], F32R)
        w_low = sb("w_low", [P, SLOTS, 2, N], F32R)
        x = sb("x", [P, TT, D])
        work = sb("work", [P, 2, N])
        ident = sb("ident", [P, P])
        ln_cols = sb("ln_cols", [P, 2 * DEPTH * 2 * KT])
        rms_cols = sb("rms_cols", [P, (B_QR + B_KVR) // P])
        stats = sb("stats", [P, TT, D // N, 6])
        moments = sb("moments", [P, TT, 2])
        var_eps = sb("var_eps", [P, TT])
        rstd = sb("rstd", [P, TT])
        minus_mean = sb("minus_mean", [P, 1])
        rms_sum = sb("rms_sum", [P, TT])
        minus_half = sb("minus_half", [P, TT])
        row_max = sb("row_max", [P, 2, TT])
        row_sum = sb("row_sum", [P, 2, TT])
        row_inv = sb("row_inv", [P, 2, TT])
        (ln_rows_end,) = overlaid(("ln_rows_end", [P, 2, D], F32))
        vb, qTn, kTn, qTr = overlaid(
            ("vb", [P, TT, B_HEADS, B_V], F32), ("qTn", [P, B_HEADS, S], F32), ("kTn", [P, B_HEADS, S], F32),
            ("qTr", [P, PAIRS, S], F32))
        xT_high = sb("xT_high", [P, KT, S], F32R)
        xT_low = sb("xT_low", [P, KT, S], F32R)
        hid_high, hid_low = overlaid(("hid_high", [P, FT, S], F32R), ("hid_low", [P, FT, S], F32R))
        room_h = 2 * FT * S
        _, ln_rows = overlaid(("ln_rows_before", [P, room_h - 2 * D], F32), ("ln_rows", [P, 2, D], F32))
        both = [("probs", [P, 2, 3 * P + 2], F32), ("probsT", [P, 2, 3 * P], F32), ("nat", [P, TT, N], F32),
                ("mixT_high", [P, KT, S], F32R), ("mixT_low", [P, KT, S], F32R)]
        with ExitStack() as shared:
            probs, probsT, nat, mixT_high, mixT_low = [shared.enter_context(nc.sbuf_tensor(*t)) for t in both]
            (cqT_high, cqT_low, ckvT_high, ckvT_low, qTa, kTa, va, kan, qn, roped, krn, kbn, kTr, dist_a, mask_b,
             cos_t, sin_t, slopes, sinks, rope_tmp, vec_rows, rms_rows) = overlaid(
                ("cqT_high", [P, B_QR // P, S], F32R), ("cqT_low", [P, B_QR // P, S], F32R),
                ("ckvT_high", [P, B_KVR // P, S], F32R), ("ckvT_low", [P, B_KVR // P, S], F32R),
                ("qTa", [P, MIX_A, S], F32), ("kTa", [P, A_KV, S], F32), ("va", [P, TT, P], F32),
                ("kan", [P, TT, A_KV, 2, A_DIM], F32), ("qn", [P, TT, 2, B_NOPE + B_ROPE], F32),
                ("roped", [P, TT, 2, B_ROPE], F32), ("krn", [P, TT, 2, B_ROPE], F32),
                ("kbn", [P, TT, 2, B_NOPE], F32), ("kTr", [P, S], F32),
                ("dist_a", [P, 3 * P], F32), ("mask_b", [P, 3 * P], F32), ("cos_t", [P, P], F32),
                ("sin_t", [P, P], F32), ("slopes", [P, A_HEADS], F32), ("sinks", [P, A_HEADS], F32),
                ("rope_tmp", [P, 4, TT, 2, B_ROPE // 2], F32), ("vec_rows", [P, P], F32),
                ("rms_rows", [(B_QR + B_KVR) // P, P], F32))
            (qTc, kTc, vc, tri, ones_late, mask_c, decay, gate_raw, gate_parts, gate_sums, log_f, log_f_high,
             log_f_low, gate_tmp, group_f, f_bias) = overlaid(
                ("qTc", [P, GH, S], F32), ("kTc", [P, GH, S], F32), ("vc", [P, TT, N], F32),
                ("tri", [P, 4 * P], F32), ("ones_late", [P, 2 * P], F32R), ("mask_c", [P, 3 * P], F32),
                ("decay", [P, 2, 2, 3, P], F32R),
                ("gate_raw", [P, KT, C_HEADS], F32), ("gate_parts", [P, KT, 2, C_HEADS], F32R),
                ("gate_sums", [P, S], F32),
                ("log_f", [P, TT, C_HEADS], F32), ("log_f_high", [P, TT, C_HEADS], F32R),
                ("log_f_low", [P, TT, C_HEADS], F32), ("gate_tmp", [P, 4, TT, C_HEADS], F32),
                ("group_f", [P, 2, TT, GH], F32), ("f_bias", [P, C_HEADS], F32))

        acc = [[ctx.enter_context(nc.psum_tensor(f"acc{s}{t}", [P, N], F32)) for t in range(TT)] for s in range(2)]
        aux = [ctx.enter_context(nc.psum_tensor(f"aux{b}", [P, N], F32)) for b in range(4)]
        SCORES, PROBS, MIX, TURN = aux

        landed = [sem(f"landed{s}") for s in range(SLOTS)]
        rounded = sem("rounded")
        cut = sem("cut")
        multiplied = sem("multiplied")
        acc_read = [sem(f"acc_read{s}") for s in range(2)]
        turned = sem("turned")
        turn_read = sem("turn_read")
        work_cut = sem("work_cut")
        work_high = sem("work_high")
        half_multiplied = sem("half_multiplied")
        end_shift = sem("end_shift")
        end_scaled = sem("end_scaled")
        end_second = sem("end_second")
        first_in = sem("first_in")
        x_landed = [sem(f"x_landed{c}") for c in range(KT // 2)]
        even_in = sem("even_in")
        odd_in = sem("odd_in")
        cols_made = sem("cols_made")
        half_set = sem("half_set")
        vector_self = sem("vector_self")
        var_ready = sem("var_ready")
        rstd_ready = sem("rstd_ready")
        squares = sem("squares")
        normed = sem("normed")
        rows_in = sem("rows_in")
        affine = sem("affine")
        pool_self = sem("pool_self")
        keys_dup = sem("keys_dup")
        rope_done = sem("rope_done")
        scores_made = sem("scores_made")
        scores_read = sem("scores_read")
        maxed = sem("maxed")
        exped = sem("exped")
        summed = sem("summed")
        probs_made = sem("probs_made")
        sink_set = sem("sink_set")
        probs_turned = sem("probs_turned")
        probsT_made = sem("probsT_made")
        mixed = sem("mixed")
        mix_rounded = sem("mix_rounded")
        mix_read = sem("mix_read")
        gate_rounded = sem("gate_rounded")
        gate_cut = sem("gate_cut")
        gates_made = sem("gates_made")
        gate_copied = sem("gate_copied")
        gates_turned = sem("gates_turned")
        values_half = sem("values_half")
        gate_bias = sem("gate_bias")
        gate_abs = sem("gate_abs")
        gate_ln = sem("gate_ln")
        forget_ready = sem("forget_ready")
        ones_ready = sem("ones_ready")
        decay_ready = sem("decay_ready")
        hid_rounded = sem("hid_rounded")
        stored = sem("stored")

        w_in_v = even_w_in[0].rearrange("(k p) n -> p k n", p=P)
        w_uq_v = even_w_uq[0].rearrange("(k p) n -> p k n", p=P)
        w_ukv_v = even_w_ukv[0].rearrange("(k p) n -> p k n", p=P)
        w_eo_v = even_w_out[0].rearrange("(k p) n -> p k n", p=P)
        w_oin_v = odd_w_in[0].rearrange("(k p) n -> p k n", p=P)
        w_oo_v = odd_w_out[0].rearrange("(k p) n -> p k n", p=P)
        w_gate_v = [ffn_w_gate[i].rearrange("(k p) n -> p k n", p=P) for i in range(DEPTH)]
        w_up_v = [ffn_w_up[i].rearrange("(k p) n -> p k n", p=P) for i in range(DEPTH)]
        w_down_v = [ffn_w_down[i].rearrange("(k p) n -> p k n", p=P) for i in range(DEPTH)]
        x_v = x_in[0].rearrange("(t p) d -> p t d", p=P)
        out_v = out[0].rearrange("(t p) d -> p t d", p=P)

        MIX_EVEN = MIX_A + B_HEADS
        HALF_UNITS = KT // 2
        DOWN_UNITS = FT // 2
        UQ_AT = PAIRS
        OUT_AT = 3 * PAIRS
        HEADS_AT = UQ_AT + 5

        END_POOL = [(1, c) for c in range(1, D // N)]
        END_VECTOR = [(0, c) for c in range(D // N)] + [(1, 0)]

        block = ctx.enter_context(nc.Block())

        @block.sync
        def _(sp):
            units = Tally()
            tallies = {"units": units}

            def fetch(src, k0, k1, cols, width):
                back = PLAN.nearest(units, "load_back")
                if back is not None:
                    sp.wait_ge(cut, units.now(1 - back))
                slot = PLAN.get(units, "load")
                sp.dma_start(raw[:, slot, 0:k1 - k0, 0:width], src[:, k0:k1, cols]).then_inc(landed[slot], 16)
                units.tick((k1 - k0) // 2)

            def strip(src, kts, cols, width=N):
                for k0 in range(0, kts, 4):
                    fetch(src, k0, min(k0 + 4, kts), cols, width)

            def ln_vectors(k, rows, to):
                sp.dma_start(to[:, 0, :], ln_gain[k // 2, k % 2:k % 2 + 1, :].to_broadcast([P, D])).then_inc(rows, 16)
                sp.dma_start(to[:, 1, :], ln_bias[k // 2, k % 2:k % 2 + 1, :].to_broadcast([P, D])).then_inc(rows, 16)

            def projection(src):
                for s in range(D // N):
                    strip(src, KT, slice(s * N, (s + 1) * N))

            def swiglu(layer):
                strip(w_gate_v[layer], KT, slice(0, N))
                sp.wait_ge(multiplied, units.now(-HALF_UNITS))
                ln_vectors(2 * layer, rows_in, ln_rows)
                strip(w_up_v[layer], KT, slice(0, N))
                with repeated(sp, tallies, 1, FSTRIPS, units=2 * HALF_UNITS) as i:
                    strip(w_gate_v[layer], KT, bass.ds(i * N, N))
                    strip(w_up_v[layer], KT, bass.ds(i * N, N))
                for s in range(D // N):
                    strip(w_down_v[layer], FT, slice(s * N, (s + 1) * N))
                    if s == 0 and layer == DEPTH - 1:
                        sp.wait_ge(multiplied, units.now(-DOWN_UNITS))
                        ln_vectors(2 * layer + 1, rows_in, ln_rows_end)

            sp.dma_start(ident[:, :], consts[:, C_ID:C_ID + P]).then_inc(first_in, 16)
            for c in range(KT // 2):
                cols = slice(2 * c * P, 2 * (c + 1) * P)
                sp.dma_start(x[:, :, cols], x_v[:, :, cols]).then_inc(x_landed[c], 16)
                if c % 2 == 0:
                    fetch(w_in_v, 2 * c, 2 * c + 4, slice(KA0, CQ0), CQ0 - KA0)
            fetch(w_in_v, 0, 4, slice(0, N), N)
            fetch(w_in_v, 4, 8, slice(0, N), N)
            n_vec = DEPTH * 2 * KT
            sp.dma_start(vec_rows[0:n_vec, :], ln_gain.rearrange("l s (k p) -> (l s k) p", p=P)).then_inc(first_in, 16)
            sp.dma_start(vec_rows[n_vec:2 * n_vec, :], ln_bias.rearrange("l s (k p) -> (l s k) p", p=P)).then_inc(first_in, 16)
            sp.dma_start(rms_rows[0:B_QR // P, :], even_q_norm.rearrange("a (k p) -> (a k) p", p=P)).then_inc(first_in, 16)
            sp.dma_start(rms_rows[B_QR // P:, :], even_kv_norm.rearrange("a (k p) -> (a k) p", p=P)).then_inc(first_in, 16)
            fetch(w_in_v, 8, 12, slice(0, N), N)
            fetch(w_in_v, 12, 16, slice(0, N), N)
            for to, at in ((dist_a, C_DA), (mask_b, C_MB), (cos_t, C_COS), (sin_t, C_SIN), (slopes, C_SL)):
                sp.dma_start(to[:, :], consts[:, at:at + to.shape[1]]).then_inc(even_in, 16)
            sp.dma_start(sinks[:, :], even_sinks[0:1, :].to_broadcast([P, A_HEADS])).then_inc(even_in, 16)
            strip(w_in_v, KT, slice(N, 2 * N))
            strip(w_in_v, KT, slice(CKV0, EVEN_IN), EVEN_IN - CKV0)
            strip(w_in_v, KT, slice(CQ0, CKV0))
            for p in range(PAIRS):
                strip(w_ukv_v, B_KVR // P, slice(p * N, (p + 1) * N))
            for p in range(PAIRS):
                strip(w_uq_v, B_QR // P, slice(p * UQW, (p + 1) * UQW), UQW)
            projection(w_eo_v)
            swiglu(0)
            strip(w_oin_v, KT, slice(0, N))
            sp.wait_ge(multiplied, units.now(-HALF_UNITS))
            ln_vectors(1, rows_in, ln_rows)
            sp.dma_start(gate_raw[:, :, :], w_oin_v[:, :, 3 * C_HD:ODD_IN]).then_inc(odd_in, 16)
            sp.dma_start(tri[:, :], consts[:, C_U:C_U + 4 * P]).then_inc(odd_in, 16)
            sp.dma_start(mask_c[:, :], consts[:, C_MC:C_MC + 3 * P]).then_inc(odd_in, 16)
            sp.dma_start(f_bias[:, :], odd_forget_bias[0:1, :].to_broadcast([P, C_HEADS])).then_inc(odd_in, 16)
            strip(w_oin_v, KT, slice(C_HD, C_HD + N))
            strip(w_oin_v, KT, slice(2 * C_HD, 2 * C_HD + N))
            with repeated(sp, tallies, 1, GROUPS, units=3 * HALF_UNITS) as i:
                for part in range(3):
                    strip(w_oin_v, KT, bass.ds(i * N + part * C_HD, N))
            projection(w_oo_v)
            swiglu(1)
            assert units.value == UNITS
            for n in range(len(END_VECTOR)):
                t, c = END_VECTOR[n]
                cols = slice(c * N, (c + 1) * N)
                sp.wait_ge(affine, 3 + n + 1)
                sp.dma_start(out_v[:, t, cols], x[:, t, cols]).then_inc(stored, 16)
                if n >= len(END_VECTOR) - len(END_POOL):
                    n -= len(END_VECTOR) - len(END_POOL)
                    t, c = END_POOL[n]
                    cols = slice(c * N, (c + 1) * N)
                    sp.wait_ge(end_second, n + 1)
                    sp.dma_start(out_v[:, t, cols], x[:, t, cols]).then_inc(stored, 16)
            sp.wait_ge(stored, 16 * TT * (D // N))

        @block.tensor
        def _(pe):
            units, turns, sets = Tally(), Tally(), [Tally(), Tally()]
            tallies = {"units": units, "turns": turns, "set0": sets[0], "set1": sets[1]}

            def products(high, low, kts, s, width=N, gap=None, half=None, lows_from=None, amid=None):
                for k in range(0, kts, 2):
                    if gap:
                        gap(k // 2)
                    pe.wait_ge(cut, units.now(1))
                    slot = PLAN.get(units, "slot")
                    for t in range(TT):
                        if k == 0 and sets[s].value:
                            pe.wait_ge(acc_read[s], sets[s].now() * TT - (TT - 1 - t))
                        rows = slice(t * P, (t + 1) * P)
                        for r in range(2):
                            for n, (a, b) in enumerate(((high, w_high), (high, w_low), (low, w_high))):
                                if n < 2 or lows_from is None:
                                    mm = pe.matmul(acc[s][t][:, 0:width], a[:, k + r, rows], b[:, slot, r, 0:width],
                                                   start=(k + r == 0 and n == 0), stop=(k + r == kts - 1 and n == 2))
                        if half and t == 0 and k + 2 == kts:
                            mm.then_inc(half, 1)
                        if amid and t == 0:
                            amid(k // 2)
                    if lows_from is not None:
                        pe.wait_ge(work_cut, lows_from + k // 2 + 1)
                        for t in range(TT):
                            for r in range(2):
                                mm = pe.matmul(acc[s][t][:, 0:width], low[:, k + r, t * P:(t + 1) * P],
                                               w_high[:, slot, r, 0:width], start=False, stop=(k + r == kts - 1))
                    mm.then_inc(multiplied, 1)
                    units.tick()
                sets[s].tick()

            def turn(pieces, bank=TURN, banks=1):
                if turns.value >= banks:
                    pe.wait_ge(turn_read, turns.now(1 - banks))
                for src, at in pieces:
                    tr = pe.transpose(bank[:, at:at + P], src, ident[:, :])
                tr.then_inc(turned, 1)
                turns.tick()

            def turn_rows(src, k0, count, **bank):
                turn([(src[:, t, (k0 + r) * P:(k0 + r + 1) * P], r * S + t * P) for r in range(count) for t in range(TT)],
                     **bank)

            def turning(chunks, cut_before, lead=3):
                def batch(b):
                    if chunks is None:
                        pe.wait_ge(x_landed[b], 16)
                    else:
                        pe.wait_ge(normed, chunks + b // 2 + 1)
                    turn_rows(x, 2 * b, 2, bank=aux[b % 4], banks=4)

                def gap(k):
                    for b in range(lead) if k == 0 else range(k + lead - 1, min(k + lead, KT // 2)):
                        batch(b)
                    pe.wait_ge(work_high, cut_before + k + 1)
                return dict(gap=gap, lows_from=cut_before)

            def scores(n, heads, first=False):
                if not first:
                    pe.wait_ge(scores_read, n)
                for t in range(TT):
                    at = slice(0, P) if t == 0 else slice(P, 3 * P)
                    for m, (q, k) in enumerate(heads):
                        mm = pe.matmul(SCORES[:, at], q[:, t * P:(t + 1) * P], k[:, 0:(t + 1) * P],
                                       start=(m == 0), stop=(m == len(heads) - 1))
                mm.then_inc(scores_made, 1)

            def turn_probs(n, parity, src, first=False):
                pe.wait_ge(probs_made, n + 1)
                if not first:
                    pe.wait_ge(probsT_made, n)
                for c in range(3):
                    tr = pe.transpose(PROBS[:, c * P:(c + 1) * P], src[:, parity, 1 + c * P:1 + (c + 1) * P], ident[:, :])
                tr.then_inc(probs_turned, 1)

            def mix(n, parity, src, values, m=None, rows=slice(0, P)):
                pe.wait_ge(probsT_made, n + 1)
                if m is not None:
                    pe.wait_ge(mix_read, m)
                pe.matmul(MIX[rows, 0:S], values[0], src[:, parity, 0:2 * P], start=True, stop=False)
                pe.matmul(MIX[rows, P:S], values[1], src[:, parity, 2 * P:3 * P], start=False, stop=True).then_inc(mixed, 1)

            def slot(s, first, count):
                h = first + s
                if s - 2 in range(count):
                    turn_probs(h - 2, h % 2, probs, first=(h == 2))
                if s < count:
                    if h < A_HEADS:
                        half = slice((h % 2) * A_DIM, (h % 2 + 1) * A_DIM)
                        heads = [(qTa[half, h // 2, :], kTa[half, h // (A_HEADS // A_KV), :])]
                    else:
                        b = h - A_HEADS
                        half = slice((b % 2) * B_ROPE, (b % 2 + 1) * B_ROPE)
                        heads = [(qTn[:, b, :], kTn[:, b, :]), (qTr[half, b // 2, :], kTr[half, :])]
                    if h % 4 == 0 or h >= A_HEADS:
                        pe.wait_ge(turn_read, turns.now())
                    scores(h, heads, first=(h == 0))
                h -= LAG
                if s - LAG in range(count):
                    if h < A_HEADS:
                        g = h // (A_HEADS // A_KV)
                        values = [va[:, t, g * A_DIM:(g + 1) * A_DIM] for t in range(TT)]
                        mix(h, h % 2, probsT, values, m=h // 2 if h % 2 == 0 and h else None,
                            rows=slice((h % 2) * A_DIM, (h % 2 + 1) * A_DIM))
                    else:
                        mix(h, h % 2, probsT, [vb[:, t, h - A_HEADS, :] for t in range(TT)], m=MIX_A + h - A_HEADS)

            pe.wait_ge(first_in, 16)
            products(xT_high, xT_low, KT, 0, CQ0 - KA0, **turning(None, 0, 2))

            def gap(k):
                if k == 3:
                    pe.wait_ge(acc_read[0], sets[0].now() * TT)
                    turn([(kan[:, t, g, :, :].rearrange("p a b -> p (a b)"), g * S + t * P)
                          for g in range(A_KV) for t in range(TT)])
                if k == 2:
                    pe.wait_ge(first_in, 16 * 5)
                    pe.transpose(MIX[:, 0:P], vec_rows[:, :], ident[:, :])
                    n_rms = (B_QR + B_KVR) // P
                    pe.transpose(MIX[:, P:P + n_rms], rms_rows[:, :], ident[0:n_rms, 0:n_rms]).then_inc(cols_made, 1)
            products(xT_high, xT_low, KT, 1, gap=gap)

            def gap(k):
                if k in (1, 2):
                    if k == 1:
                        pe.wait_ge(acc_read[1], sets[1].now() * TT)
                    turn_rows(nat, 2 * (k - 1), 2)
                if k >= 3:
                    if k == 3:
                        pe.wait_ge(half_set, 1)
                    slot(k - 3, 0, A_HEADS)
            products(xT_high, xT_low, KT, 0, gap=gap)

            def gap(k):
                slot(5 + k, 0, A_HEADS)
                if k in (1, 2):
                    if k == 1:
                        pe.wait_ge(acc_read[0], sets[0].now() * TT)
                    turn_rows(nat, 2 * (k - 1), 2)
            products(xT_high, xT_low, KT, 1, EVEN_IN - CKV0, gap)

            def gap(k):
                if k < 6:
                    slot(13 + k, 0, A_HEADS)
                if k == 3:
                    pe.wait_ge(acc_read[1], sets[1].now() * TT)
                    turn_rows(nat, 0, 2)
            products(xT_high, xT_low, KT, 0, gap=gap)

            def late(t):
                if t - HEADS_AT in range(B_HEADS + LAG - 1):
                    slot(t - HEADS_AT, A_HEADS, B_HEADS)
                rows = roped[:, :, :, :].rearrange("p t a b -> p t (a b)")
                if t == 1:
                    pe.wait_ge(rope_done, 1)
                    turn([(rows[:, u, :], u * P) for u in range(TT)])
                if t - 2 in range(PAIRS):
                    pe.wait_ge(acc_read[(t - 1) % 2], sets[(t - 1) % 2].now() * TT)
                    turn([(kbn[:, u, j, :], j * S + u * P) for j in range(2) for u in range(TT)])
                if t in (2, 3):
                    if t == 2:
                        pe.wait_ge(acc_read[0], TT * 3)
                    turn_rows(nat, 2 * (t - 2), 2, bank=PROBS, banks=2)
                p, odd = (t - UQ_AT - 3) // 2, (t - UQ_AT - 3) % 2
                if p in range(PAIRS) and not odd:
                    pe.wait_ge(acc_read[(p + 1) % 2], TT * (5 + (p + 1) // 2))
                    turn([(qn[:, u, j, 0:B_NOPE], j * S + u * P) for j in range(2) for u in range(TT)])
                if p in range(PAIRS) and odd:
                    pe.wait_ge(rope_done, p + 2)
                    turn([(rows[:, u, :], u * P) for u in range(TT)])

            pe.wait_ge(keys_dup, 1)
            for p in range(PAIRS):
                if p == 0:
                    pe.wait_ge(work_cut, KT // 2 + 1)
                products(ckvT_high, ckvT_low, B_KVR // P, (p + 1) % 2, gap=lambda k: late(p))

            def latent_gap(k, p):
                late(UQ_AT + 2 * p + k)
                if p == 0 and k == 0:
                    pe.wait_ge(work_cut, KT // 2 + 3)
            for p in range(PAIRS):
                products(cqT_high, cqT_low, B_QR // P, (p + 1) % 2, UQW, lambda k: latent_gap(k, p))

            def projection(outputs, flip, beside, amid=None):
                for s in range(D // N):
                    def gap(k):
                        if s == 0:
                            beside(k)
                            pe.wait_ge(mix_read, outputs + 2 * (k + 1))
                    products(mixT_high, mixT_low, KT, (s + flip) % 2, gap=gap, half=half_multiplied, amid=None if s else amid)

            def swiglu(layer, chunks, cut_before):
                def gap(k):
                    if k in (2, 3):
                        if k == 2:
                            pe.wait_ge(acc_read[1], sets[1].now() * TT)
                        turn_rows(work, 2 * (k - 2), 2, bank=aux[k - 2], banks=2)

                def strips(before):
                    products(xT_high, xT_low, KT, 0, **(dict(gap=gap) if before else turning(chunks, cut_before)))
                    products(xT_high, xT_low, KT, 1)

                strips(False)
                with repeated(pe, tallies, 1, FSTRIPS, units=2 * HALF_UNITS, set0=1, set1=1, turns=2):
                    strips(True)

                def first_gap(k):
                    gap(k)
                    if k == (FT - N // P) // 2:
                        pe.wait_ge(turn_read, turns.now())
                for s in range(D // N):
                    products(hid_high, hid_low, FT, s % 2, gap=None if s else first_gap, half=half_multiplied)


            def amid(k):
                if OUT_AT + k - HEADS_AT == B_HEADS + LAG - 2:
                    slot(B_HEADS + LAG - 1, A_HEADS, B_HEADS)
            projection(0, 1, lambda k: late(OUT_AT + k), amid)
            swiglu(0, 0, KT // 2 + 3)

            def odd_slot(s, i):
                n0 = HEADS_EVEN + i * GH
                if s - 2 in range(GH):
                    turn_probs(n0 + (s - 2), s % 2, probs)
                if s < GH:
                    n, par = n0 + s, s % 2
                    pe.wait_ge(scores_read, n)
                    pe.wait_ge(decay_ready, i * GH + (s + 1))
                    if s == 0:
                        pe.wait_ge(ones_ready, 1)
                    if s == 0:
                        pe.wait_ge(turn_read, turns.now())
                    late, ones = ones_late[:, P:2 * P], ones_late[:, :]
                    for m in range(2):
                        pe.matmul(SCORES[:, 0:P], decay[:, par, m, 0, :], late, start=(m == 0), stop=False)
                    pe.matmul(SCORES[:, 0:P], qTc[:, s, 0:P], kTc[:, s, 0:P], start=False, stop=True)
                    for m in range(2):
                        pe.matmul(SCORES[:, P:3 * P], decay[:, par, m, 2, :], ones, start=(m == 0), stop=False)
                        pe.matmul(SCORES[:, P:2 * P], decay[:, par, m, 1, :], late, start=False, stop=False)
                    pe.matmul(SCORES[:, P:3 * P], qTc[:, s, P:S], kTc[:, s, :], start=False, stop=True).then_inc(scores_made, 1)
                if s - LAG in range(GH):
                    j = s - LAG
                    if j == 0:
                        pe.wait_ge(acc_read[0], sets[0].now() * TT)
                    mix(n0 + j, j % 2, probsT, [vc[:, t, j * C_DIM:(j + 1) * C_DIM] for t in range(TT)],
                        m=MIX_EVEN + i * GH + j)

            def gate_products():
                pe.wait_ge(gate_cut, 1)
                for k in range(KT):
                    pe.matmul(MIX[0:2 * C_HEADS, 0:S], gate_parts[:, k, :, :].rearrange("p a b -> p (a b)"),
                              xT_high[:, k, :], start=(k == 0), stop=False)
                for k in range(KT):
                    mm = pe.matmul(MIX[0:C_HEADS, 0:S], gate_parts[:, k, 0, :], xT_low[:, k, :],
                                   start=False, stop=(k == KT - 1))
                mm.then_inc(gates_made, 1)

            def gate_rows():
                pe.wait_ge(gate_copied, 1)
                for t in range(TT):
                    for m in range(2):
                        mm = pe.matmul(MIX[:, S + t * C_HEADS:S + (t + 1) * C_HEADS],
                                       gate_sums[0:2 * C_HEADS, t * P:(t + 1) * P],
                                       ident[0:2 * C_HEADS, m * C_HEADS:(m + 1) * C_HEADS], start=(m == 0), stop=(m == 1))
                mm.then_inc(gates_turned, 1)

            def group(i, first):
                def gap(k):
                    if k % 2 == 1:
                        odd_slot(k // 2, i - 1)
                products(xT_high, xT_low, KT, 0, **(turning(D // N, KT + 3) if first else dict(gap=gap)))

                def gap(k):
                    if first and k == 6:
                        gate_products()
                    if first and k == 7:
                        gate_rows()
                    if not first and k in (1, 3, 5):
                        odd_slot(4 + k // 2, i - 1)
                    if k in (2, 4):
                        if k == 2:
                            pe.wait_ge(acc_read[0], sets[0].now() * TT)
                        turn_rows(nat, k - 2, 2)
                products(xT_high, xT_low, KT, 1, gap=gap)

                def gap(k):
                    if k in (2, 4):
                        if k == 2:
                            pe.wait_ge(acc_read[1], sets[1].now() * TT)
                        turn_rows(nat, k - 2, 2)
                products(xT_high, xT_low, KT, 0, gap=gap, half=values_half)

            group(0, True)
            with repeated(pe, tallies, 1, GROUPS, units=3 * HALF_UNITS, set0=2, set1=1, turns=4) as i:
                group(i, False)

            projection(MIX_EVEN, 0, lambda k: odd_slot(k, GROUPS - 1))
            swiglu(1, 2 * (D // N), 3 * KT // 2 + 3)

        @block.scalar
        def _(act):
            units, turns, z = Tally(), Tally(), Tally()
            seen = [Tally() for _ in range(SLOTS)]
            tallies = {"units": units, "turns": turns, "z": z} | {f"seen{s}": t for s, t in enumerate(seen)}
            SEEN = {f"seen{s}": 1 for s in range(SLOTS)}

            def round_ahead(more=AHEAD):
                if units.value + more >= UNITS:
                    return
                load, half = PLAN.get(units, "load", more), PLAN.get(units, "half", more)
                slot, width = PLAN.get(units, "slot", more), PLAN.get(units, "width", more)
                if half == 0:
                    seen[load].tick()
                    act.wait_ge(landed[load], seen[load].now() * 16)
                back = PLAN.nearest(units, "back", more)
                if back is not None:
                    act.wait_ge(multiplied, units.now(more + 1 - back))
                act.copy(w_high[:, slot, :, 0:width], raw[:, load, 2 * half:2 * half + 2, 0:width]).then_inc(rounded, 1)

            def unit():
                round_ahead()
                units.tick()

            def strip_done(k):
                act.wait_ge(multiplied, units.now(-k))

            def turn_read_to(out_ap, bank=TURN, width=N, dims=None):
                act.wait_ge(turned, turns.now(1))
                src = bank[:, 0:width]
                if dims:
                    src = src.rearrange("p (a b) -> p a b", a=dims)
                act.copy(out_ap, src).then_inc(turn_read, 1)
                turns.tick()

            def turn_to_work(bank, gain=None, bias=None):
                act.wait_ge(turned, turns.now(1))
                if z.value >= 2:
                    act.wait_ge(work_cut, z.now(-1))
                to = work[:, z.value % 2, :]
                if gain is None:
                    op = act.copy(to, bank[:, :])
                else:
                    for r in range(2):
                        part = slice(r * S, (r + 1) * S)
                        op = act.activation(to[:, part], bank[:, part], ACT.Identity, scale=gain[:, r:r + 1],
                                            bias=bias[:, r:r + 1] if bias is not None else 0.0)
                op.then_inc(turn_read, 1)
                turns.tick()
                z.tick()

            def turning(k, norm, lead=3):
                for b in range(lead) if k < 0 else range(k + lead - 1, min(k + lead, KT // 2)) if k else ():
                    if norm is None:
                        turn_to_work(aux[b % 4])
                    else:
                        at, bias_at = norm * KT + 2 * b, (2 * DEPTH + norm) * KT + 2 * b
                        turn_to_work(aux[b % 4], ln_cols[:, at:at + 2], ln_cols[:, bias_at:bias_at + 2])

            def exp_rows(n, parity, src, sink):
                act.wait_ge(maxed, n + 1)
                for t, (a, b) in enumerate(((0 if sink else 1, P + 1), (P + 1, 3 * P + (2 if sink else 1)))):
                    op = act.activation(src[:, parity, a:b], src[:, parity, a:b], ACT.Exp,
                                        bias=row_max[:, parity, t:t + 1], accum_out=row_sum[:, parity, t:t + 1])
                op.then_inc(exped, 1)

            def probs_copy(n, parity, to, first=False):
                act.wait_ge(probs_turned, n + 1)
                if not first:
                    act.wait_ge(mixed, n - 1)
                act.copy(to[:, parity, :], PROBS[:, 0:3 * P]).then_inc(probsT_made, 1)

            def mix_round(n, to):
                act.wait_ge(mixed, n + 1)
                act.copy(to, MIX[:, 0:S]).then_inc(mix_rounded, 1)

            def slot(s, first, count):
                h = first + s
                if s - 2 in range(count):
                    probs_copy(h - 2, h % 2, probsT, first=(h - 2 < 2))
                h -= LAG
                if s - LAG in range(count) and (h >= A_HEADS or h % 2 == 1):
                    mix_round(h, mixT_high[:, MIX_A + h - A_HEADS if h >= A_HEADS else h // 2, :])
                h += LAG
                if s < count:
                    exp_rows(h, h % 2, probs, h < A_HEADS)

            def rms_squares(s, width):
                for t, spare in enumerate((kbn, qn)):
                    op = act.activation(spare[:, :, :, :].rearrange("p a b c -> p (a b c)")[:, 0:width],
                                        acc[s][t][:, 0:width], ACT.Square, accum_out=rms_sum[:, t:t + 1])
                op.then_inc(squares, 1)

            for b in range(AHEAD):
                if b < 2:
                    turn_to_work(aux[b])
                round_ahead(b)
            for k in range(HALF_UNITS):
                unit()
                turning(k, None, 2)
            for k in range(HALF_UNITS):
                unit()
                if k == 0:
                    strip_done(1)
                    for t in range(TT):
                        for dup in range(2):
                            act.copy(kan[:, t, :, dup, :], acc[0][t][:, 0:P].rearrange("p (g d) -> p g d", g=A_KV))
                        act.copy(va[:, t, :], acc[0][t][:, P:2 * P]).then_inc(acc_read[0], 1)
                if k == 3:
                    turn_read_to(kTa[:, :, :], dims=A_KV)
                if k == 2:
                    act.wait_ge(cols_made, 1)
                    act.copy(ln_cols[:, :], MIX[:, 0:P])
                    act.copy(rms_cols[:, :], MIX[:, P:P + (B_QR + B_KVR) // P]).then_inc(half_set, 1)
            act.wait_ge(half_set, 1)
            for k in range(HALF_UNITS):
                unit()
                if k == 0:
                    strip_done(1)
                    for t in range(TT):
                        act.mul(nat[:, t, :], acc[1][t][:, :], A_DIM ** -0.5).then_inc(acc_read[1], 1)
                if k in (1, 2):
                    turn_read_to(qTa[:, 2 * (k - 1):2 * k, :], dims=2)
                if k >= 3:
                    slot(k - 3, 0, A_HEADS)
            for k in range(HALF_UNITS):
                unit()
                if k == 0:
                    strip_done(1)
                    for t in range(TT):
                        act.mul(nat[:, t, :], acc[0][t][:, :], A_DIM ** -0.5).then_inc(acc_read[0], 1)
                slot(5 + k, 0, A_HEADS)
                if k in (1, 2):
                    turn_read_to(qTa[:, 2 + 2 * k:4 + 2 * k, :], dims=2)
            for k in range(HALF_UNITS):
                unit()
                if k == 0:
                    strip_done(1)
                    rms_squares(1, B_KVR)
                    for t in range(TT):
                        for dup in range(2):
                            op = act.copy(krn[:, t, dup, :], acc[1][t][:, B_KVR:B_KVR + B_ROPE])
                    op.then_inc(keys_dup, 1)
                if k < 6:
                    slot(13 + k, 0, A_HEADS)
                if k == 3:
                    turn_to_work(TURN, rms_cols[:, B_QR // P:(B_QR + B_KVR) // P])

            def late(t):
                if t - HEADS_AT in range(B_HEADS + LAG - 1):
                    slot(t - HEADS_AT, A_HEADS, B_HEADS)
                if t - HEADS_AT == B_HEADS + LAG - 2:
                    slot(t - HEADS_AT + 1, A_HEADS, B_HEADS)
                if t == 0:
                    strip_done(1)
                    act.wait_ge(acc_read[1], TT * 2)
                    rms_squares(0, B_QR)
                if t == 1:
                    turn_read_to(kTr[:, :], width=S)
                if t - 2 in range(PAIRS):
                    turn_read_to(kTn[:, 2 * (t - 2):2 * (t - 1), :], dims=2)
                if t in (2, 3):
                    turn_to_work(PROBS, rms_cols[:, 2 * (t - 2):2 * (t - 1)])
                p, odd = (t - UQ_AT - 3) // 2, (t - UQ_AT - 3) % 2
                if p in range(PAIRS) and not odd:
                    turn_read_to(qTn[:, 2 * p:2 * p + 2, :], dims=2)
                if p in range(PAIRS) and odd:
                    turn_read_to(qTr[:, p, :], width=S)
                if t - 1 in range(PAIRS):
                    p = t - 1
                    strip_done(1)
                    if p == 0:
                        act.wait_ge(squares, 2)
                    both_kv = acc[(p + 1) % 2][0][:, :].rearrange("p (j c) -> p j c", j=2)
                    act.copy(kbn[:, 0, :, :], both_kv[:, :, 0:B_NOPE])
                    act.copy(vb[:, 0, 2 * p:2 * p + 2, :], both_kv[:, :, B_NOPE:]).then_inc(acc_read[(p + 1) % 2], 1)
                p, odd = (t - UQ_AT - 2) // 2, (t - UQ_AT - 2) % 2
                if p in range(PAIRS) and not odd:
                    strip_done(1)
                    if p:
                        act.wait_ge(rope_done, p + 1)
                    for u in range(TT):
                        act.mul(qn[:, u, :, :], acc[(p + 1) % 2][u][:, 0:UQW].rearrange("p (j c) -> p j c", j=2),
                                (B_NOPE + B_ROPE) ** -0.5).then_inc(acc_read[(p + 1) % 2], 1)

            for t in range(OUT_AT):
                unit()
                late(t)

            def projection(beside):
                for s in range(D // N):
                    for k in range(HALF_UNITS):
                        unit()
                        if s == 0:
                            beside(k)

            def swiglu(layer):
                def hidden_round(i):
                    for b in range(2):
                        act.wait_ge(turned, turns.now(1))
                        act.copy(hid_high[:, bass.ds(i * 4 + 2 * b, 2), :] if not isinstance(i, int)
                                 else hid_high[:, 4 * i + 2 * b:4 * i + 2 * b + 2, :],
                                 aux[b][:, :].rearrange("p (a b) -> p a b", a=2)).then_inc(hid_rounded, 1)
                        turns.tick()

                def strips(i, before):
                    if not before:
                        turning(-1, 2 * layer)
                    for k in range(HALF_UNITS):
                        unit()
                        if not before:
                            turning(k, 2 * layer)
                        if before and k == 3:
                            hidden_round(i - 1)
                    for k in range(HALF_UNITS):
                        unit()
                        if k == 0:
                            strip_done(1)
                            act.wait_ge(turned, turns.now())
                            for t in range(TT):
                                act.activation(work[:, t, :], acc[0][t][:, :], ACT.Silu).then_inc(acc_read[0], 1)

                strips(0, False)
                act.wait_ge(affine, 2 * layer + 1)
                with repeated(act, tallies, 1, FSTRIPS, units=2 * HALF_UNITS, turns=2,
                              **{k: 2 * v for k, v in SEEN.items()}) as i:
                    strips(i, True)
                for k in range(D // N * DOWN_UNITS):
                    unit()
                    if k == 3:
                        hidden_round(FSTRIPS - 1)

            projection(lambda k: late(OUT_AT + k))
            swiglu(0)

            def odd_slot(s, i):
                n0 = HEADS_EVEN + i * GH
                if s - 2 in range(GH):
                    probs_copy(n0 + (s - 2), s % 2, probsT)
                if s - LAG in range(GH):
                    m = i * GH + (s - LAG)
                    to = mixT_high[:, m, :] if isinstance(i, int) else \
                        mixT_high[:, bass.ds(m, 1), :].rearrange("p a b -> p (a b)")
                    mix_round(n0 + (s - LAG), to)
                if s < GH:
                    exp_rows(n0 + s, s % 2, probs, False)

            def values_out(i):
                act.wait_ge(values_half, i + 1)
                act.copy(vc[:, 0, :], acc[0][0][:, :]).then_inc(acc_read[0], 1)
                act.wait_ge(multiplied, units.now())
                act.copy(vc[:, 1, :], acc[0][1][:, :]).then_inc(acc_read[0], 1)

            def group(i, first):
                if first:
                    turning(-1, 1)
                for k in range(HALF_UNITS):
                    unit()
                    if first:
                        turning(k, 1)
                    if not first and k % 2 == 1:
                        odd_slot(k // 2, i - 1)
                for k in range(HALF_UNITS):
                    unit()
                    if k == 0:
                        strip_done(1)
                        act.wait_ge(turned, turns.now())
                        for t in range(TT):
                            act.mul(nat[:, t, :], acc[0][t][:, :], C_DIM ** -0.5).then_inc(acc_read[0], 1)
                    if not first and k in (1, 3, 5):
                        odd_slot(4 + k // 2, i - 1)
                    if k in (2, 4):
                        turn_read_to(qTc[:, k - 2:k, :], dims=2)
                    if first and k == 4:
                        act.wait_ge(odd_in, 16 * 4)
                        act.copy(gate_parts[:, :, 0, :], gate_raw[:, :, :]).then_inc(gate_rounded, 1)
                    if first and k == 6:
                        act.wait_ge(gates_made, 1)
                        act.copy(gate_sums[0:2 * C_HEADS, :], MIX[0:2 * C_HEADS, 0:S]).then_inc(gate_copied, 1)
                    if first and k == 7:
                        log_sigmoid()
                for k in range(HALF_UNITS):
                    unit()
                    if k == 0:
                        strip_done(1)
                        act.wait_ge(turned, turns.now())
                        for t in range(TT):
                            act.copy(nat[:, t, :], acc[1][t][:, :]).then_inc(acc_read[1], 1)
                    if k in (2, 4):
                        turn_read_to(kTc[:, k - 2:k, :], dims=2)
                values_out(i)

            def log_sigmoid():
                act.wait_ge(gate_bias, 1)
                act.activation(gate_tmp[:, 1, :, :], gate_tmp[:, 0, :, :], ACT.Abs).then_inc(gate_abs, 1)
                act.wait_ge(gate_abs, 1)
                act.activation(gate_tmp[:, 2, :, :], gate_tmp[:, 1, :, :], ACT.Exp, scale=-1.0).then_inc(gate_abs, 1)
                act.wait_ge(gate_abs, 2)
                act.activation(gate_tmp[:, 3, :, :], gate_tmp[:, 2, :, :], ACT.Ln, bias=1.0).then_inc(gate_ln, 1)

            group(0, True)
            with repeated(act, tallies, 1, GROUPS, units=3 * HALF_UNITS, turns=4,
                          **{k: 3 * v for k, v in SEEN.items()}) as i:
                group(i, False)

            projection(lambda k: odd_slot(k, GROUPS - 1))
            swiglu(1)
            act.wait_ge(end_shift, 1)
            for t, c in END_POOL:
                cols = slice(c * N, (c + 1) * N)
                act.activation(x[:, t, cols], x[:, t, cols], ACT.Identity, scale=rstd[:, 1:2],
                               bias=minus_mean[:, 0:1]).then_inc(end_scaled, 1)

        @block.vector
        def _(dve):
            units, turns, z, own, hids, halves = (Tally() for _ in range(6))
            sums_of = [Tally(), Tally()]
            tallies = {"units": units, "turns": turns, "z": z, "own": own, "hids": hids, "halves": halves,
                       "acc0": sums_of[0], "acc1": sums_of[1]}

            def cut_ahead(more=AHEAD):
                if units.value + more >= UNITS:
                    return
                load, half = PLAN.get(units, "load", more), PLAN.get(units, "half", more)
                slot, width = PLAN.get(units, "slot", more), PLAN.get(units, "width", more)
                dve.wait_ge(rounded, units.now(more + 1))
                dve.tensor_tensor(w_low[:, slot, :, 0:width], raw[:, load, 2 * half:2 * half + 2, 0:width],
                                  w_high[:, slot, :, 0:width].bitcast(F32), ALU.subtract).then_inc(cut, 1)

            def unit():
                cut_ahead()
                units.tick()

            def strip_done(k):
                dve.wait_ge(multiplied, units.now(-k))

            def result(op):
                op.then_inc(vector_self, 1)
                own.tick()
                dve.wait_ge(vector_self, own.now())

            def work_to(high, low):
                turns.tick()
                src = work[:, z.value % 2, :].rearrange("p (a b) -> p a b", a=2)
                dve.wait_ge(turn_read, turns.now())
                dve.tensor_copy(high, src).then_inc(work_high, 1)
                dve.wait_ge(work_high, z.now(1))
                dve.tensor_tensor(low, src, high.bitcast(F32), ALU.subtract).then_inc(work_cut, 1)
                z.tick()

            def residual(s, cols, at, k):
                for t in range(TT):
                    if t == 0:
                        halves.tick()
                        dve.wait_ge(half_multiplied, halves.now())
                    else:
                        dve.wait_ge(multiplied, units.now(-k))
                    dve.scalar_tensor_tensor(out=x[:, t, cols], in0=x[:, t, cols], scalar=ALPHA, in1=acc[s][t][:, :],
                                             op0=ALU.mult, op1=ALU.add).then_inc(acc_read[s], 1)
                    sums_of[s].tick()
                    dve.wait_ge(acc_read[s], sums_of[s].now())
                    dve.bn_stats(stats[:, t, at, :], x[:, t, cols]).then_inc(vector_self, 1)
                    own.tick()

            def projection(count_units, norm, flip=0, heads=None, beside=None):
                for s in range(D // N):
                    for k in range(count_units - (s == D // N - 1)):
                        if s == 0 and heads:
                            heads(k)
                        unit()
                        if s == 0 and beside:
                            beside(k)
                        if s and k == 0:
                            residual((s - 1 + flip) % 2, slice((s - 1) * N, s * N), s - 1, 1)
                last_residual((s + flip) % 2, slice(s * N, D), s, norm)

            def last_residual(s, cols, at, norm):
                def add(t):
                    dve.scalar_tensor_tensor(out=x[:, t, cols], in0=x[:, t, cols], scalar=ALPHA, in1=acc[s][t][:, :],
                                             op0=ALU.mult, op1=ALU.add).then_inc(acc_read[s], 1)
                    sums_of[s].tick()

                def counted(op):
                    op.then_inc(vector_self, 1)
                    own.tick()

                def statistics(t):
                    dve.wait_ge(acc_read[s], sums_of[s].now())
                    counted(dve.bn_stats(stats[:, t, at, :], x[:, t, cols]))

                def aggregate(t):
                    dve.wait_ge(vector_self, own.now())
                    counted(dve.bn_aggr(moments[:, t, :], stats[:, t, :, :].rearrange("p a b -> p (a b)")))

                def variance(t):
                    dve.tensor_scalar(var_eps[:, t:t + 1], moments[:, t, 1:2], LN_EPS, None, ALU.add).then_inc(var_ready, 1)

                halves.tick()
                dve.wait_ge(half_multiplied, halves.now())
                add(0)
                statistics(0)
                dve.wait_ge(multiplied, units.now(1))
                add(1)
                aggregate(0)
                statistics(1)
                dve.wait_ge(vector_self, own.now(-1))
                variance(0)
                aggregate(1)
                dve.wait_ge(vector_self, own.now())
                variance(1)

            def normalise_half(c, t):
                cols = slice(c * N, (c + 1) * N)
                return dve.tensor_scalar(x[:, t, cols], x[:, t, cols], moments[:, t, 0:1], rstd[:, t:t + 1],
                                         ALU.subtract, ALU.mult)

            def normalise_chunk(c):
                for t in range(TT):
                    op = normalise_half(c, t)
                op.then_inc(normed, 1)

            def x_to(b):
                work_to(xT_high[:, 2 * b:2 * b + 2, :], xT_low[:, 2 * b:2 * b + 2, :])

            def turning(k, norm, lead=3):
                if k < 0:
                    for t in range(TT):
                        dve.wait_ge(rstd_ready, 3 + TT * norm + t)
                        op = normalise_half(0, t)
                    op.then_inc(normed, 1)
                    normalise_chunk(1)
                    x_to(0)
                    unit()
                    for b in range(1, lead):
                        x_to(b)
                    normalise_chunk(2)
                    normalise_chunk(3)
                elif k and k + lead - 1 < KT // 2:
                    x_to(k + lead - 1)

            def read_scores(n, parity, to, bias, slope=None, first=False):
                dve.wait_ge(scores_made, n + 1)
                if not first:
                    dve.wait_ge(probs_turned, n - 1)
                if slope is not None:
                    op = dve.scalar_tensor_tensor(out=to[:, parity, 1:3 * P + 1], in0=bias, scalar=slope,
                                                  in1=SCORES[:, 0:3 * P], op0=ALU.mult, op1=ALU.add)
                else:
                    op = dve.tensor_tensor(to[:, parity, 1:3 * P + 1], SCORES[:, 0:3 * P], bias, ALU.add)
                op.then_inc(scores_read, 1)
                dve.wait_ge(scores_read, n + 1)
                sink = slope is not None
                if sink:
                    dve.wait_ge(sink_set, n + 1)
                for t, (a, b) in enumerate(((0 if sink else 1, P + 1), (P + 1, 3 * P + (2 if sink else 1)))):
                    op = dve.tensor_reduce(row_max[:, parity, t:t + 1], to[:, parity, a:b], AX_X, ALU.max, negate=True)
                op.then_inc(maxed, 1)

            def normalise(n, parity, to):
                dve.wait_ge(exped, n + 1)
                dve.reciprocal(row_inv[:, parity, :], row_sum[:, parity, :]).then_inc(summed, 1)
                dve.wait_ge(summed, n + 1)
                for t, (a, b) in enumerate(((1, P + 1), (P + 1, 3 * P + 1))):
                    op = dve.tensor_scalar(to[:, parity, a:b], to[:, parity, a:b], row_inv[:, parity, t:t + 1], None, ALU.mult)
                op.then_inc(probs_made, 1)

            def mix_low(m, high, low):
                dve.wait_ge(mix_rounded, m + 1)
                dve.tensor_tensor(low, MIX[:, 0:S], high.bitcast(F32), ALU.subtract).then_inc(mix_read, 1)

            def rms(s, width, round_no):
                dve.wait_ge(squares, round_no)
                dve.tensor_scalar(var_eps[:, :], rms_sum[:, :], 1.0 / width, RMS_EPS, ALU.mult, ALU.add).then_inc(var_ready, 1)
                dve.wait_ge(turned, turns.now())
                dve.wait_ge(rstd_ready, round_no)
                if round_no == 1:
                    dve.wait_ge(keys_dup, 1)
                for t in range(TT):
                    dve.tensor_scalar(nat[:, t, 0:width], acc[s][t][:, 0:width], rstd[:, t:t + 1], None,
                                      ALU.mult).then_inc(acc_read[s], 1)

            def softmax(s, first, count):
                h = first + s
                if s - 1 in range(count):
                    normalise(h - 1, (h - 1) % 2, probs)
                if s in range(count):
                    if h < A_HEADS:
                        read_scores(h, h % 2, probs, dist_a[:, :], slopes[:, h:h + 1], first=(h < 2))
                    else:
                        read_scores(h, h % 2, probs, mask_b[:, :])

            def outputs(s, first, count):
                h = first + s - LAG
                if s - LAG in range(count) and (h >= A_HEADS or h % 2 == 1):
                    m = MIX_A + h - A_HEADS if h >= A_HEADS else h // 2
                    mix_low(m, mixT_high[:, m, :], mixT_low[:, m, :])

            for b in range(AHEAD):
                if b < 2:
                    x_to(b)
                cut_ahead(b)
            for k in range(HALF_UNITS):
                unit()
                turning(k, None, 2)
            for k in range(HALF_UNITS):
                unit()
                if k == 3:
                    turns.tick()
            dve.wait_ge(even_in, 16 * 6)
            for k in range(HALF_UNITS):
                softmax(k - 3, 0, A_HEADS)
                unit()
                if k in (1, 2):
                    turns.tick()
                outputs(k - 3, 0, A_HEADS)
            for k in range(HALF_UNITS):
                softmax(5 + k, 0, A_HEADS)
                unit()
                outputs(5 + k, 0, A_HEADS)
                if k in (1, 2):
                    turns.tick()
            for k in range(HALF_UNITS):
                softmax(13 + k, 0, A_HEADS)
                unit()
                outputs(13 + k, 0, A_HEADS)
                if k == 0:
                    rms(1, B_KVR, 1)
                if k == 3:
                    work_to(ckvT_high[:, :, :], ckvT_low[:, :, :])

            def late(t):
                if t - HEADS_AT in range(B_HEADS + LAG - 1):
                    outputs(t - HEADS_AT, A_HEADS, B_HEADS)
                if t - HEADS_AT == B_HEADS + LAG - 2:
                    outputs(t - HEADS_AT + 1, A_HEADS, B_HEADS)
                if t == 0:
                    rms(0, B_QR, 2)
                if t == 1:
                    turns.tick()
                if t - 2 in range(PAIRS):
                    turns.tick()
                if t - 1 in range(PAIRS):
                    p = t - 1
                    strip_done(1)
                    if p == 0:
                        dve.wait_ge(squares, 2)
                    else:
                        dve.wait_ge(turned, turns.now())
                    both_kv = acc[(p + 1) % 2][1][:, :].rearrange("p (j c) -> p j c", j=2)
                    dve.tensor_copy(kbn[:, 1, :, :], both_kv[:, :, 0:B_NOPE])
                    dve.tensor_copy(vb[:, 1, 2 * p:2 * p + 2, :], both_kv[:, :, B_NOPE:]).then_inc(acc_read[(p + 1) % 2], 1)
                if t in (2, 3):
                    b = 2 * (t - 2)
                    work_to(cqT_high[:, b:b + 2, :], cqT_low[:, b:b + 2, :])
                if t - UQ_AT - 3 in range(2 * PAIRS):
                    turns.tick()

            for t in range(OUT_AT):
                softmax(t - HEADS_AT, A_HEADS, B_HEADS)
                unit()
                late(t)
            sums_of[0].value = TT * (3 + PAIRS)
            sums_of[1].value = TT * (2 + PAIRS)

            def swiglu(layer):
                def hidden_low(i):
                    for b in range(2):
                        dve.wait_ge(hid_rounded, hids.now(1))
                        at = slice(4 * i + 2 * b, 4 * i + 2 * b + 2) if isinstance(i, int) else bass.ds(i * 4 + 2 * b, 2)
                        dve.tensor_tensor(hid_low[:, at, :], aux[b][:, :].rearrange("p (a b) -> p a b", a=2),
                                          hid_high[:, at, :].bitcast(F32), ALU.subtract).then_inc(turn_read, 1)
                        hids.tick()
                        turns.tick()

                def gate_up(k):
                    dve.wait_ge(acc_read[0], sums_of[0].now(TT))
                    strip_done(k)
                    for t in range(TT):
                        dve.tensor_tensor(work[:, t, :], acc[1][t][:, :], work[:, t, :], ALU.mult).then_inc(acc_read[1], 1)
                    sums_of[0].tick(TT)
                    sums_of[1].tick(TT)

                def strips(i, before):
                    if not before:
                        turning(-1, 2 * layer)
                    for k in range(HALF_UNITS):
                        unit()
                        if not before:
                            turning(k, 2 * layer)
                        if before and k == 0:
                            gate_up(1)
                        if before and k == 3:
                            hidden_low(i - 1)
                    for k in range(HALF_UNITS):
                        unit()
                strips(0, False)
                dve.wait_ge(affine, 2 * layer + 1)
                with repeated(dve, tallies, 1, FSTRIPS, units=2 * HALF_UNITS, turns=2, hids=2, acc0=TT, acc1=TT) as i:
                    strips(i, True)

                def beside(k):
                    if k == 0:
                        gate_up(1)
                    if k == 3:
                        hidden_low(FSTRIPS - 1)
                projection(DOWN_UNITS, 2 * layer + 1, beside=beside)

            projection(HALF_UNITS, 0, 1, lambda k: softmax(OUT_AT + k - HEADS_AT, A_HEADS, B_HEADS), lambda k: late(OUT_AT + k))
            swiglu(0)

            def odd_softmax(s, i):
                n0 = HEADS_EVEN + i * GH
                if s - 1 in range(GH):
                    normalise(n0 + (s - 1), (s - 1) % 2, probs)
                if s < GH:
                    read_scores(n0 + s, s % 2, probs, mask_c[:, :])

            def odd_outputs(s, i):
                if s - LAG in range(GH):
                    m = i * GH + (s - LAG)
                    high, low = (w[:, m, :] if isinstance(i, int) else
                                 w[:, bass.ds(m, 1), :].rearrange("p a b -> p (a b)") for w in (mixT_high, mixT_low))
                    mix_low(m + MIX_EVEN, high, low)

            def group(i, first):
                if first:
                    turning(-1, 1)
                for k in range(HALF_UNITS):
                    if not first and k % 2 == 1:
                        odd_softmax(k // 2, i - 1)
                    unit()
                    if first:
                        turning(k, 1)
                    if not first and k % 2 == 1:
                        odd_outputs(k // 2, i - 1)
                for k in range(HALF_UNITS):
                    if not first and k in (1, 3, 5):
                        odd_softmax(4 + k // 2, i - 1)
                    unit()
                    if not first and k in (1, 3, 5):
                        odd_outputs(4 + k // 2, i - 1)
                    if first and k == 4:
                        dve.wait_ge(gate_rounded, 1)
                        dve.tensor_tensor(gate_parts[:, :, 1, :], gate_raw[:, :, :], gate_parts[:, :, 0, :].bitcast(F32),
                                          ALU.subtract).then_inc(gate_cut, 1)
                        dve.tensor_copy(ones_late[:, :], tri[:, P:3 * P]).then_inc(ones_ready, 1)
                    if first and k == 7:
                        forget_gates()
                for k in range(HALF_UNITS):
                    unit()

            def forget_gates():
                dve.wait_ge(gates_turned, 1)
                sums_ap = MIX[:, S:S + TT * C_HEADS].rearrange("p (t h) -> p t h", t=TT)
                for t in range(TT):
                    op = dve.tensor_tensor(gate_tmp[:, 0, t, :], sums_ap[:, t, :], f_bias[:, :], ALU.add)
                op.then_inc(gate_bias, 1)
                dve.wait_ge(gate_bias, 1)
                result(dve.tensor_scalar(log_f[:, :, :], gate_tmp[:, 0, :, :], 0.0, None, ALU.min))
                dve.wait_ge(gate_ln, 1)
                result(dve.tensor_tensor(log_f[:, :, :], log_f[:, :, :], gate_tmp[:, 3, :, :], ALU.subtract))
                result(dve.tensor_copy(log_f_high[:, :, :], log_f[:, :, :]))
                dve.tensor_tensor(log_f_low[:, :, :], log_f[:, :, :], log_f_high[:, :, :].bitcast(F32),
                                  ALU.subtract).then_inc(forget_ready, 1)

            group(0, True)
            with repeated(dve, tallies, 1, GROUPS, units=3 * HALF_UNITS) as i:
                group(i, False)
            turns.tick(4 * GROUPS)
            sums_of[0].tick(2 * TT * GROUPS)
            sums_of[1].tick(TT * GROUPS)
            dve.wait_ge(affine, 2)

            projection(HALF_UNITS, 2, 0, lambda k: odd_softmax(k, GROUPS - 1), lambda k: odd_outputs(k, GROUPS - 1))
            swiglu(1)
            units.tick()
            dve.wait_ge(rstd_ready, 2 + 2 * DEPTH * TT)
            dve.tensor_scalar(minus_mean[:, :], moments[:, 1, 0:1], rstd[:, 1:2], -1.0, ALU.mult, ALU.mult).then_inc(end_shift, 1)
            dve.wait_ge(rows_in, 32 * 4)

            def gained(t, c):
                cols = slice(c * N, (c + 1) * N)
                dve.scalar_tensor_tensor(out=x[:, t, cols], in0=x[:, t, cols], scalar=moments[:, t, 0:1],
                                         in1=ln_rows_end[:, 0, cols], op0=ALU.subtract, op1=ALU.mult).then_inc(vector_self, 1)
                own.tick()

            gained(*END_VECTOR[0])
            for n in range(len(END_VECTOR)):
                t, c = END_VECTOR[n]
                cols = slice(c * N, (c + 1) * N)
                ahead = n + 1 < len(END_VECTOR)
                if ahead:
                    gained(*END_VECTOR[n + 1])
                dve.wait_ge(vector_self, own.now(-ahead))
                dve.scalar_tensor_tensor(out=x[:, t, cols], in0=x[:, t, cols], scalar=rstd[:, t:t + 1],
                                         in1=ln_rows_end[:, 1, cols], op0=ALU.mult, op1=ALU.add).then_inc(affine, 1)

        @block.gpsimd
        def _(pool):
            own = Tally()

            def result(op):
                op.then_inc(pool_self, 1)
                own.tick()
                pool.wait_ge(pool_self, own.now())

            def inverse_root(n):
                pool.wait_ge(var_ready, n)
                pool.tensor_tensor(rstd[:, :], var_eps[:, :], minus_half[:, :], ALU.pow).then_inc(rstd_ready, 1)

            def inverse_halves(norm):
                for t in range(TT):
                    pool.wait_ge(var_ready, 3 + TT * norm + t)
                    pool.tensor_tensor(rstd[:, t:t + 1], var_eps[:, t:t + 1], minus_half[:, t:t + 1],
                                       ALU.pow).then_inc(rstd_ready, 1)

            def rotate(src):
                h = B_ROPE // 2
                x1, x2 = src[:, :, :, 0:h], src[:, :, :, h:B_ROPE]
                cos, sin = (c[:, :].rearrange("p (t j h) -> p t j h", t=TT, j=2) for c in (cos_t, sin_t))
                for k, (a, b) in enumerate(((x1, cos), (x2, sin), (x2, cos), (x1, sin))):
                    op = pool.tensor_tensor(rope_tmp[:, k, :, :, :], a, b, ALU.mult)
                result(op)
                pool.tensor_tensor(roped[:, :, :, 0:h], rope_tmp[:, 0, :, :, :], rope_tmp[:, 1, :, :, :], ALU.subtract)
                pool.tensor_tensor(roped[:, :, :, h:B_ROPE], rope_tmp[:, 2, :, :, :], rope_tmp[:, 3, :, :, :], ALU.add)\
                    .then_inc(rope_done, 1)

            def affine_rows(k, turned_before):
                pool.wait_ge(rows_in, 32 * (k + 1))
                pool.wait_ge(turned, turned_before)
                for t in range(TT):
                    op = pool.tensor_tensor(x[:, t, :], x[:, t, :], ln_rows[:, 0, :], ALU.mult)
                result(op)
                for t in range(TT):
                    op = pool.tensor_tensor(x[:, t, :], x[:, t, :], ln_rows[:, 1, :], ALU.add)
                op.then_inc(affine, 1)

            pool.memset(minus_half[:, :], -0.5).then_inc(pool_self, 1)
            own.tick()
            pool.wait_ge(pool_self, 1)
            def set_sink(s):
                if s >= 2:
                    pool.wait_ge(probs_turned, s - 1)
                pool.tensor_copy(probs[:, s % 2, 0:1], sinks[:, s:s + 1])
                pool.tensor_copy(probs[:, s % 2, 3 * P + 1:3 * P + 2], sinks[:, s:s + 1]).then_inc(sink_set, 1)

            pool.wait_ge(even_in, 16 * 6)
            for s in range(14):
                set_sink(s)
            inverse_root(1)
            set_sink(14)
            set_sink(15)
            pool.wait_ge(keys_dup, 1)
            rotate(krn)
            inverse_root(2)
            KEYS_TURNED = KT // 2 + 1 + 2 + 2 + 1 + 1
            PAIR_TURNED = KEYS_TURNED + PAIRS + 2
            for p in range(PAIRS):
                pool.wait_ge(acc_read[(p + 1) % 2], TT * (5 + (p + 1) // 2))
                pool.wait_ge(turned, PAIR_TURNED + 2 * p if p else KEYS_TURNED)
                rotate(qn[:, :, :, B_NOPE:])
            inverse_halves(0)
            turns = PAIR_TURNED + 2 * PAIRS + KT // 2
            affine_rows(0, turns)
            inverse_halves(1)
            turns += 2 * FSTRIPS + KT // 2
            affine_rows(1, turns)

            pool.wait_ge(forget_ready, 1)

            def decays(i):
                group = slice(GH * i, GH * (i + 1)) if isinstance(i, int) else bass.ds(i * GH, GH)
                pool.tensor_copy(group_f[:, 0, :, :], log_f_high[:, :, group].bitcast(F32))
                result(pool.tensor_copy(group_f[:, 1, :, :], log_f_low[:, :, group]))
                for j in range(GH):
                    pool.wait_ge(scores_made, HEADS_EVEN + i * GH + (j - 1))
                    for m in range(2):
                        pool.tensor_tensor(decay[:, j % 2, m, 0:2, :].rearrange("p a b -> p (a b)"), tri[:, 0:2 * P],
                                           group_f[:, m, 0, j:j + 1].to_broadcast([P, 2 * P]), ALU.mult)
                        op = pool.tensor_tensor(decay[:, j % 2, m, 2, :], tri[:, 0:P],
                                                group_f[:, m, 1, j:j + 1].to_broadcast([P, P]), ALU.mult)
                    op.then_inc(decay_ready, 1)
                pool.wait_ge(decay_ready, i * GH + GH)

            with repeated(pool, {"own": own}, 0, GROUPS, own=1) as i:
                decays(i)
            inverse_halves(2)
            turns += 4 * GROUPS + KT // 2
            affine_rows(2, turns)
            inverse_halves(3)
            pool.wait_ge(rows_in, 32 * 4)

            def gained(n):
                t, c = END_POOL[n]
                cols = slice(c * N, (c + 1) * N)
                pool.wait_ge(end_scaled, n + 1)
                pool.tensor_tensor(x[:, t, cols], x[:, t, cols], ln_rows_end[:, 0, cols], ALU.mult).then_inc(pool_self, 1)
                own.tick()

            gained(0)
            for n in range(len(END_POOL)):
                t, c = END_POOL[n]
                cols = slice(c * N, (c + 1) * N)
                ahead = n + 1 < len(END_POOL)
                if ahead:
                    gained(n + 1)
                pool.wait_ge(pool_self, own.now(-ahead))
                pool.tensor_tensor(x[:, t, cols], x[:, t, cols], ln_rows_end[:, 1, cols], ALU.add).then_inc(end_second, 1)


_INS = ["x", "even_w_in", "even_sinks", "even_q_norm", "even_w_uq", "even_kv_norm", "even_w_ukv", "even_w_out",
        "odd_w_in", "odd_forget_bias", "odd_w_out", "ffn_w_gate", "ffn_w_up", "ffn_w_down", "ln_gain", "ln_bias"]


def kernel(**inputs):
    import concourse.bacc as _bacc
    from concourse.bass_utils import run_bass_kernel_spmd as _run

    nc = _bacc.Bacc("TRN2", target_bir_lowering=False, num_devices=1)
    arrays = {f"in_{name}": np.ascontiguousarray(inputs[name]) for name in _INS}
    arrays["in_constants"] = constants()
    args = [nc.dram_tensor(n, a.shape, mybir.dt.from_np(a.dtype), kind="ExternalInput").ap() for n, a in arrays.items()]
    out = nc.dram_tensor("out_0", (1, S, D), F32, kind="ExternalOutput").ap()
    trunk(nc, *args, out)
    r = _run(nc, [arrays], core_ids=[0])
    return r.results[0]["out_0"]
```
